# Optimizing a Trainium2 kernel written in Bass

```python
import jax, jax.numpy as jnp
from jax import lax
import numpy as np

D_MODEL = 1024
BATCH = 1
SEQ = 512
DEPTH = 2
DEC_BATCH = 8
DEC_SEQ = 4
PAST_LEN = 4096
PAGE_SIZE = 128

N_MIXERS = 2
N_A = (DEPTH + 1) // 2
N_B = DEPTH // 2
H_A = 8
DV_A = D_MODEL // H_A
DK_A = DV_A // 2
CHUNK_A = 64
IN_A = 2 * H_A * DK_A + 2 * D_MODEL + 2 * H_A
CONV_W = 3
D_FF = 4 * D_MODEL
N_MOD = 6
EPS = 1e-6

kernel_name = "mlstm_shortconv_hybrid_step"

def rmsnorm(x, g):
    xf = x.astype(jnp.float32)
    y = xf * lax.rsqrt(jnp.mean(xf * xf, axis=-1, keepdims=True) + EPS)
    return y.astype(x.dtype) * g

def modulate(x, g, shift, scale):
    return rmsnorm(x, g) * (1 + scale[:, None, :]) + shift[:, None, :]

def mlstm_chunk(carry, xs):
    C0, n0, m0 = carry
    q, k, v, ig, lf = xs
    L = q.shape[2]
    b = jnp.cumsum(lf, axis=-1)
    causal = jnp.tril(jnp.ones((L, L), dtype=bool))
    dmat = jnp.where(causal, b[..., :, None] - b[..., None, :] + ig[..., None, :], -jnp.inf)
    inter = b + m0[..., None]
    m = jnp.maximum(inter, jnp.max(dmat, axis=-1))
    s = jnp.einsum('bhtd,bhsd->bhts', q, k) * jnp.exp(dmat - m[..., None])
    e_inter = jnp.exp(inter - m)
    num = jnp.einsum('bhts,bhse->bhte', s, v) + e_inter[..., None] * jnp.einsum('bhtd,bhde->bhte', q, C0)
    den = jnp.sum(s, axis=-1) + e_inter * jnp.einsum('bhtd,bhd->bht', q, n0)
    h = num / jnp.maximum(jnp.abs(den), jnp.exp(-m))[..., None]
    m_l = m[..., -1]
    a = jnp.exp(b[..., -1:] - b + ig - m_l[..., None])
    decay = jnp.exp(b[..., -1] + m0 - m_l)
    C1 = decay[..., None, None] * C0 + jnp.einsum('bhs,bhsd,bhse->bhde', a, k, v)
    n1 = decay[..., None] * n0 + jnp.einsum('bhs,bhsd->bhd', a, k)
    return (C1, n1, m_l), h

def mlstm_mixer(h, C0, n0, m0, w_in, b_gates, g_head, w_out):
    bn, t, _ = h.shape
    hk = H_A * DK_A
    p = (h @ w_in).astype(jnp.float32)
    q = p[..., :hk]
    k = p[..., hk:2 * hk] * (DK_A ** -0.5)
    v = p[..., 2 * hk:2 * hk + D_MODEL]
    o = p[..., 2 * hk + D_MODEL:2 * hk + 2 * D_MODEL]
    gates = p[..., 2 * hk + 2 * D_MODEL:] + b_gates.astype(jnp.float32)
    ig = gates[..., :H_A]
    lf = jax.nn.log_sigmoid(gates[..., H_A:])
    L = CHUNK_A if t % CHUNK_A == 0 else t
    nc = t // L

    def heads(z, d):
        return z.reshape(bn, t, H_A, d).transpose(0, 2, 1, 3)

    def chunks(z):
        return jnp.moveaxis(z.reshape(bn, H_A, nc, L, *z.shape[3:]), 2, 0)

    xs = (chunks(heads(q, DK_A)), chunks(heads(k, DK_A)), chunks(heads(v, DV_A)),
          chunks(ig.transpose(0, 2, 1)), chunks(lf.transpose(0, 2, 1)))
    init = (C0.astype(jnp.float32), n0.astype(jnp.float32), m0.astype(jnp.float32))
    (C1, n1, m1), hs = lax.scan(mlstm_chunk, init, xs)
    hs = jnp.moveaxis(hs, 0, 2).reshape(bn, H_A, t, DV_A)
    hs = hs * lax.rsqrt(jnp.mean(hs * hs, axis=-1, keepdims=True) + EPS)
    hs = hs.transpose(0, 2, 1, 3).reshape(bn, t, D_MODEL)
    y = (hs * g_head.astype(jnp.float32) * jax.nn.sigmoid(o)).astype(h.dtype)
    return y @ w_out, C1.astype(h.dtype), n1.astype(h.dtype), m1.astype(h.dtype)

def conv_mixer(h, buf, w_in, w_conv, w_out):
    t = h.shape[1]
    p = h @ w_in
    bg = p[..., :D_MODEL]
    cg = p[..., D_MODEL:2 * D_MODEL]
    xt = p[..., 2 * D_MODEL:]
    u = cg * xt
    full = jnp.concatenate([buf.astype(u.dtype), u], axis=1)
    y = w_conv[0] * full[:, 0:t]
    for j in range(1, CONV_W):
        y = y + w_conv[j] * full[:, j:j + t]
    return (bg * y) @ w_out, full[:, t:]

def trunk(x, c, C0s, n0s, m0s, bufs, ada_w, ada_b, norm_g, final_norm_g,
          mlstm_w_in, mlstm_b_gates, mlstm_head_g, mlstm_w_out,
          conv_w_in, conv_w, conv_w_out, mlp_w_up, mlp_w_down):
    new_C, new_n, new_m, new_buf = [], [], [], []
    for i in range(DEPTH):
        mod = (jax.nn.silu(c) @ ada_w[i] + ada_b[i]).reshape(c.shape[0], N_MOD, D_MODEL)
        hn = modulate(x, norm_g[i, 0], mod[:, 0], mod[:, 1])
        j = i // N_MIXERS
        if i % N_MIXERS == 0:
            out, C1, n1, m1 = mlstm_mixer(hn, C0s[j], n0s[j], m0s[j], mlstm_w_in[j],
                                          mlstm_b_gates[j], mlstm_head_g[j], mlstm_w_out[j])
            new_C.append(C1)
            new_n.append(n1)
            new_m.append(m1)
        else:
            out, b1 = conv_mixer(hn, bufs[j], conv_w_in[j], conv_w[j], conv_w_out[j])
            new_buf.append(b1)
        x = x + mod[:, 2][:, None, :] * out
        hn = modulate(x, norm_g[i, 1], mod[:, 3], mod[:, 4])
        f = jnp.square(jax.nn.relu(hn @ mlp_w_up[i])) @ mlp_w_down[i]
        x = x + mod[:, 5][:, None, :] * f
    return (rmsnorm(x, final_norm_g), jnp.stack(new_C), jnp.stack(new_n),
            jnp.stack(new_m), jnp.stack(new_buf))

def setup_inputs(seed: int = 0) -> dict:
    key = jax.random.key(seed)
    ks = jax.random.split(key, 24)

    def nrm(k, shape, s):
        return jax.random.normal(k, shape, jnp.float32) * s

    d = D_MODEL
    return {
        "x_prompt": nrm(ks[0], (BATCH, SEQ, d), 1.0),
        "x_sample": nrm(ks[1], (DEC_BATCH, DEC_SEQ, d), 1.0),
        "c_prompt": nrm(ks[2], (BATCH, d), 1.0),
        "c_sample": nrm(ks[3], (DEC_BATCH, d), 1.0),
        "state_mlstm_C": nrm(ks[4], (N_A, DEC_BATCH, H_A, DK_A, DV_A), DK_A ** -0.5),
        "state_mlstm_n": nrm(ks[5], (N_A, DEC_BATCH, H_A, DK_A), DK_A ** -0.5),
        "state_mlstm_m": nrm(ks[6], (N_A, DEC_BATCH, H_A), 1.0),
        "state_conv": nrm(ks[7], (N_B, DEC_BATCH, CONV_W - 1, d), 1.0),
        "ada_w": nrm(ks[8], (DEPTH, d, N_MOD * d), d ** -0.5),
        "ada_b": nrm(ks[9], (DEPTH, N_MOD * d), 0.02),
        "norm_g": 1.0 + nrm(ks[10], (DEPTH, 2, d), 0.02),
        "final_norm_g": 1.0 + nrm(ks[11], (d,), 0.02),
        "mlstm_w_in": nrm(ks[12], (N_A, d, IN_A), d ** -0.5),
        "mlstm_b_gates": jnp.concatenate([nrm(ks[13], (N_A, H_A), 0.1),
                                          3.0 + nrm(ks[14], (N_A, H_A), 0.1)], axis=-1),
        "mlstm_head_g": 1.0 + nrm(ks[15], (N_A, d), 0.02),
        "mlstm_w_out": nrm(ks[16], (N_A, d, d), d ** -0.5),
        "conv_w_in": nrm(ks[17], (N_B, d, 3 * d), d ** -0.5),
        "conv_w": nrm(ks[18], (N_B, CONV_W, d), CONV_W ** -0.5),
        "conv_w_out": nrm(ks[19], (N_B, d, d), d ** -0.5),
        "mlp_w_up": nrm(ks[20], (DEPTH, d, D_FF), d ** -0.5),
        "mlp_w_down": nrm(ks[21], (DEPTH, D_FF, d), D_FF ** -0.5),
    }

def reference(x_prompt, x_sample, c_prompt, c_sample, state_mlstm_C, state_mlstm_n,
              state_mlstm_m, state_conv, ada_w, ada_b, norm_g, final_norm_g,
              mlstm_w_in, mlstm_b_gates, mlstm_head_g, mlstm_w_out,
              conv_w_in, conv_w, conv_w_out, mlp_w_up, mlp_w_down):
    dt = x_prompt.dtype
    bp = x_prompt.shape[0]
    zC = jnp.zeros((N_A, bp, H_A, DK_A, DV_A), dt)
    zn = jnp.zeros((N_A, bp, H_A, DK_A), dt)
    zm = jnp.zeros((N_A, bp, H_A), dt)
    zb = jnp.zeros((N_B, bp, CONV_W - 1, D_MODEL), dt)
    y_prompt, prompt_C, prompt_n, prompt_m, prompt_conv = trunk(
        x_prompt, c_prompt, zC, zn, zm, zb, ada_w, ada_b, norm_g, final_norm_g,
        mlstm_w_in, mlstm_b_gates, mlstm_head_g, mlstm_w_out,
        conv_w_in, conv_w, conv_w_out, mlp_w_up, mlp_w_down)
    y_sample, sample_C, sample_n, sample_m, sample_conv = trunk(
        x_sample, c_sample, state_mlstm_C, state_mlstm_n, state_mlstm_m, state_conv,
        ada_w, ada_b, norm_g, final_norm_g,
        mlstm_w_in, mlstm_b_gates, mlstm_head_g, mlstm_w_out,
        conv_w_in, conv_w, conv_w_out, mlp_w_up, mlp_w_down)
    return (y_prompt, y_sample, prompt_C, prompt_n, prompt_m, prompt_conv,
            sample_C, sample_n, sample_m, sample_conv)


_drawn_inputs = setup_inputs


def setup_inputs(seed=0):
    import zlib

    import numpy as np

    out = dict(_drawn_inputs(seed))
    spreads = {}
    factors = {'final_norm_g': 2.752, 'mlstm_head_g': 6.181}
    for name, (base, spread) in spreads.items():
        noise = np.random.default_rng([zlib.crc32(name.encode()), seed]).standard_normal(out[name].shape)
        drawn = base * np.exp(spread * noise) if base else spread * noise
        out[name] = __import__('jax').numpy.asarray(drawn.astype(out[name].dtype))
    for name, factor in factors.items():
        out[name] = (out[name] * factor).astype(out[name].dtype)
    return out
```

```python
import concourse.bass as bass
from concourse import mybir
from contextlib import ExitStack

F32 = mybir.dt.float32
F32R = mybir.dt.float32r
ALU = mybir.AluOpType
ACT = mybir.ActivationFunctionType
AX = mybir.AxisListType

P = 128
D = 1024
KT = D // P
SEQ, SB, ST = 512, 8, 4
PH, SH = SEQ // 2, SB * ST // 2
HALF = PH + SH
TOK = 2 * HALF
NS = SB * ST
NSEQ = 1 + SB
H, DK, DV = 8, 64, 128
DVA = DV + 1
NJ = SEQ // P
EPS = 1e-6
SLOTS, LEAD = 4, 3
NMOD = 6
DFF = 4 * D
QUARTERS = DFF // D
CONVW = 3
UROW = 2 + SEQ + SB * (2 + ST)
LAST_COL = HALF + PH - 1

T_ADA0, T_ADA1 = 0, 8
T_QK, T_V, T_O, T_WOUT = 16, 32, 48, 64
T_MLP0, T_MLP0_LAST = 80, 176
T_CG, T_XT, T_BG, T_COUT = 192, 200, 208, 216
T_MLP1, T_MLP1_LAST, T_END = 224, 272, 288
G_QK, G_V, G_O, G_WOUT, G_MLP0, G_MLP0_LAST = 0, 8, 16, 24, 32, 80
G_CG, G_XT, G_BG, G_COUT, G_MLP1, G_MLP1_LAST = 96, 104, 112, 120, 128, 176
X_NORM0, X_Y, X_NORM1, X_NORM2, X_NORM3 = 0, 8, 16, 24, 32


class Count:

    def __init__(self, engine, sem):
        self.engine, self.sem, self.n = engine, sem, 0

    def link(self, ins):
        ins.then_inc(self.sem, 1)
        self.n += 1
        self.engine.wait_ge(self.sem, self.n)


def halves(ap):
    return ap.rearrange("p (h c) -> p h c", h=2)


def prompt(ap):
    return halves(ap)[:, :, 0:PH]


def sample(ap):
    return halves(ap)[:, :, PH:HALF]


def sample4(ap):
    return sample(ap).rearrange("p h (b t) -> p h b t", t=ST)


def col(t):
    return (t // PH) * HALF + t % PH


def build_program(nc, ins, outs):
    ctx = ExitStack()
    with ctx:
        base = (nc.sbuf_base + 63) // 64 * 64
        mark = {"at": base}

        def sb(name, shape, dt=F32, at=None):
            n = 4
            for s in shape[1:]:
                n *= s
            n = (n + 31) // 32 * 32
            if at is None:
                at = mark["at"]
                mark["at"] += n
            return nc.alloc_sbuf_tensor_at(name, shape, dt, offset=at)

        def region(nbytes):
            at = mark["at"]
            mark["at"] += (nbytes + 31) // 32 * 32
            return at

        def sem(name):
            return ctx.enter_context(nc.semaphore(name))

        ROW = TOK * 4
        at_x = region(KT * ROW)
        xT = sb("xT", [P, KT, TOK], at=at_x)
        NUMB = 2080
        PW = sum(SEQ - P * j for j in range(NJ))
        probs = [sb(f"probs{i}", [P, PW], at=at_x + i * PW * 4) for i in range(2)]
        num = [sb(f"num{i}", [P, NJ, DVA], at=at_x + 2 * PW * 4 + i * NUMB) for i in range(2)]
        ktok_s = sb("ktok_s", [NS, H * DK], at=at_x + 2 * PW * 4 + 2 * NUMB)
        at_s = at_x
        dec_s = sb("dec_s", [NS, H, NS], at=at_s)
        negM_s = sb("negM_s", [NS, H, NS], at=at_s + 1024)
        probs_s = sb("probs_s", [NS, H, 2 * NS], at=at_s + 2048)
        einter_s = sb("einter_s", [P, H // 2, NS], at=at_s + 4096)
        kam = sb("kam", [NS, SB, P], at=at_s + 4608)
        num_s = sb("num_s", [2 * NS, H // 2, DVA], at=at_x + 2 * PW * 4)
        Xh = sb("Xh", [P, KT, TOK], F32R)
        Xl = sb("Xl", [P, KT, TOK], F32R)
        at_h = region(2 * KT * ROW)
        Hh = sb("Hh", [P, KT, TOK], F32R, at=at_h)
        Hl = sb("Hl", [P, KT, TOK], F32R, at=at_h + KT * ROW)
        xin = sb("xin", [P, NJ + 1, D], at=at_h)
        vtok = sb("vtok", [P, NJ, H, DVA], at=at_h)
        C0 = sb("C0", [P, SB, H // 2, DVA], at=at_h + NJ * H * DVA * 4)
        at_t = at_h + (NJ + SB // 2) * H * DVA * 4
        qs = sb("qs", [P, H // 2, NS], at=at_t)
        ks = sb("ks", [P, H // 2, NS], at=at_t + 512)
        tok = sb("tok", [P, 3, NJ, H], at=at_t + 1024)
        yrow = sb("yrow", [P, NJ, D], at=at_h)
        yrow_s = sb("yrow_s", [SH, 2, D], at=at_h + NJ * D * 4)
        raw = sb("raw", [P, SLOTS, KT, P])
        wh = sb("wh", [P, SLOTS, KT, P], F32R)
        wl = sb("wl", [P, SLOTS, KT, P], F32R)
        modT = sb("modT", [P, 2 * NMOD, KT, NSEQ])
        gain = sb("gain", [P, KT, NSEQ])
        par0 = sb("par0", [P, P])
        par1 = sb("par1", [P, 40])
        ident = sb("ident", [P, P])
        ones = sb("ones", [P, P])
        c2 = sb("c2", [P, KT, 2 * NSEQ], F32R)
        at_row = region(D * 4)
        modrow = sb("modrow", [2 * NSEQ, D], at=at_row)
        sel = sb("sel", [H, H, P], at=at_row)
        modps = sb("modps", [P, KT, 2 * NSEQ])
        modsum = sb("modsum", [P, KT, NSEQ])
        stage = [sb(f"stage{i}", [P, TOK]) for i in range(2)]
        vs = [sb(f"vs{i}", [P, NS]) for i in range(2)]
        at_sq = region(ROW)
        sqb = sb("sqb", [P, TOK], at=at_sq)
        hs = sb("hs", [P, NJ, DV], at=at_sq)
        small_s = sb("small_s", [P, SH * 2])
        g_s = sb("g_s", [NS, H])
        a_s = sb("a_s", [NS, H])
        enm_s = sb("enm_s", [2 * NS, H // 2])
        stat = sb("stat", [P, 6, NJ])
        mhalf = sb("mhalf", [P, NJ])
        mask_b = sb("mask_b", [NS, SB])
        bgate = sb("bgate", [P, 1])
        m0row = sb("m0row", [H, SB])
        epsc = sb("epsc", [P, 1])
        at_n = region(5 * ROW)
        rstd = sb("rstd", [P, TOK], at=at_n)
        acc = sb("acc", [P, TOK], at=at_n + ROW)
        xr = sb("xr", [P, TOK], at=at_n + 2 * ROW)
        hb = [sb(f"hb{i}", [P, TOK], at=at_n + (3 + i) * ROW) for i in range(2)]
        qbd = sb("qbd", [P, H // 2, SB, 2 * NS], at=at_n)
        negMp = sb("negMp", [H, SEQ], at=at_n + 8192)
        Cp = sb("Cp", [DK, H, DVA], at=at_n)
        at_f = region(2 * 4 * ROW + KT * ROW + NJ * H * DK * 4)
        qT = sb("qT", [P, H // 2, TOK], at=at_f)
        kT = sb("kT", [P, H // 2, TOK], at=at_f + 4 * ROW)
        og = sb("og", [P, KT, TOK], at=at_f + 8 * ROW)
        ktok = sb("ktok", [P, NJ, H * DK], at=at_f + 16 * ROW)
        vtok_s = sb("vtok_s", [NS, H, DVA])
        rows = [sb(f"rows{i}", [H, TOK], at=at_f + 8 * ROW + i * ROW) for i in range(6)]
        gw = 8 * 40 * 4
        graw = sb("graw", [P, KT, 40], at=at_f + 14 * ROW)
        gh = sb("gh", [P, KT, 40], F32R, at=at_f + 14 * ROW + gw)
        gl = sb("gl", [P, KT, 40], F32R, at=at_f + 14 * ROW + 2 * gw)
        crow = sb("crow", [NSEQ, 3, D], at=at_f)
        parrow0 = sb("parrow0", [P, P], at=at_f + 12288)
        parrow1 = sb("parrow1", [40, P], at=at_f + 12288 + 512)
        ccol = sb("ccol", [P, KT, NSEQ], at=at_f + 12288 + 1024)
        u = sb("u", [P, KT, UROW], at=at_f)
        yc = sb("yc", [P, KT, TOK], at=at_f + KT * UROW * 4)
        crows = sb("crows", [2 * SB, D], at=at_f + KT * UROW * 4 + KT * ROW)
        urows = sb("urows", [2 * NSEQ, D], at=at_f + KT * UROW * 4 + KT * ROW)
        ulast = sb("ulast", [P, KT, 2 * NSEQ], at=at_f + KT * UROW * 4 + KT * ROW + D * 4)
        assert mark["at"] <= nc.sbuf_usable_end, mark["at"] - nc.sbuf_usable_end

        G = ctx.enter_context(nc.psum_tensor("G", [P, 4, 512], F32))
        B4, B5, B6, B7 = [ctx.enter_context(nc.psum_tensor(f"B{i}", [P, 512], F32)) for i in range(4, 8)]

        def slot(g):
            return G[:, 2 * (g % 2):2 * (g % 2) + 2, 0:HALF]

        xspill = nc.dram_tensor("xspill", [P, KT * TOK], F32, kind="Internal").ap()
        bounce = nc.dram_tensor("bounce", [5, H, NS], F32, kind="Internal").ap()

        s_raw = [sem(f"raw_in{i}") for i in range(SLOTS)]
        s_hi = sem("hi_ready")
        s_lo = [sem("lo_even"), sem("lo_odd")]
        s_used = sem("tile_used")
        s_ev = sem("evacuated")
        s_dr = sem("drained")
        s_mid = sem("drain_mid")
        s_ae = sem("ada_pair_out")
        s_at = sem("ada_cols")
        s_tr = sem("ada_turned")
        s_cmb = sem("ada_mid")
        s_mod = sem("mod_ready")
        s_kx = sem("x_operand")
        s_hh = sem("norm_h")
        s_hhi = sem("norm_hi")
        s_vt = sem("kv_turned")
        s_vtd = sem("kv_turned_out")
        s_stat = sem("stat_sum")
        s_root = sem("stat_root")
        s_acc = sem("squares_summed")
        s_v, s_a, s_p = sem("vector_chain"), sem("scalar_chain"), sem("gpsimd_chain")
        s_cin, s_xin, s_pin, s_gin, s_sin = sem("c_in"), sem("x_in"), sem("params_in"), sem("gates_in"), sem("state_in")
        s_const = sem("constants")
        s_silu = sem("silu_ready")
        s_ct, s_cs, s_pt, s_ptd = sem("c_turned"), sem("c_split"), sem("params_turned"), sem("params_out")
        s_xt, s_xe, s_xst, s_xse = sem("x_turned"), sem("x_stored"), sem("xs_turned"), sem("xs_stored")
        s_gs = sem("gates_split")
        s_gp, s_rv, s_ra = sem("gates_product"), sem("rows_vector"), sem("rows_scalar")
        s_spill, s_back = sem("x_spilled"), sem("x_back")
        s_bo, s_bi = sem("bounce_out"), sem("bounce_in")
        s_tt, s_ttd = sem("rows_turned"), sem("rows_turned_out")
        s_sd, s_sp = sem("sample_decay"), sem("sample_vector")
        s_ssc, s_spv, s_sht, s_snum = sem("sample_scores"), sem("sample_pv"), sem("sample_turned"), sem("sample_num")
        s_srs = sem("sample_rs")
        s_kam, s_cu, s_cud = sem("kam_ready"), sem("state_product"), sem("state_updated")
        s_selr = sem("selector")
        s_bc, s_s, s_d, s_sel, s_pr = sem("negM_spread"), sem("scores"), sem("decay"), sem("masked"), sem("probs_ready")
        s_pv, s_num, s_sq, s_rs, s_hs = sem("pv"), sem("num_out"), sem("squares"), sem("head_rs"), sem("hs_ready")
        s_ht, s_y, s_yh = sem("hs_turned"), sem("y_ready"), sem("y_hi")
        s_cp, s_cpo = sem("prompt_state"), sem("prompt_state_out")
        s_out = sem("stored")
        s_crin, s_crt, s_cre = sem("conv_rows_in"), sem("conv_rows_turned"), sem("conv_rows_out")
        s_ul, s_ult, s_ulo = sem("u_last"), sem("u_last_turned"), sem("u_last_out")
        s_fy, s_ft, s_fo = sem("final_y"), sem("final_turned"), sem("final_out")
        n_out = {"n": 0}

        ctx.enter_context(nc.allow_non_contiguous_dma(reason="a few small loads of single elements"))
        block = ctx.enter_context(nc.Block())

        def at(n, j, per):
            return n if j is None else j * per + n

        def split_wait(eng, t, j, per):
            eng.wait_ge(s_hi, at(t + 1, j, per))
            eng.wait_ge(s_lo[t % 2], at(t // 2 + 1, j, per // 2))

        @block.sync
        def _(sp):
            def fetch(t, w, c, j=None, per=0):
                if t >= SLOTS:
                    sp.wait_ge(s_lo[t % 2], at((t - SLOTS) // 2 + 1, j, per // 2))
                nc.sync.dma_start(raw[:, t % SLOTS], w.rearrange("(k p) n -> p k n", p=P)[:, :, bass.ds(c, P)])\
                    .then_inc(s_raw[t % SLOTS], 16)

            def unit(t0, w, c0, j=None, per=0):
                for m in range(KT):
                    fetch(t0 + m, w, c0 + P * m, j, per)

            def mixed(t0, w, c0, wa, ca, j=None, per=0):
                for m in range(0, KT, 2):
                    for i in range(2):
                        fetch(t0 + 2 * m + i, wa, ca + P * (m + i), j, per)
                    for i in range(2):
                        fetch(t0 + 2 * m + 2 + i, w, c0 + P * (m + i), j, per)

            ada = [ins["ada_w"][layer] for layer in range(2)]
            w_in, w_out = ins["mlstm_w_in"][0], ins["mlstm_w_out"][0]
            unit(T_ADA0, ada[0], 0)
            unit(T_ADA1, ada[0], D)
            mixed(T_QK, w_in, 0, ada[0], 2 * D)
            mixed(T_V, w_in, D, ada[0], 3 * D)
            mixed(T_O, w_in, 2 * D, ada[0], 4 * D)
            mixed(T_WOUT, w_out, 0, ada[0], 5 * D)
            up, down = ins["mlp_w_up"], ins["mlp_w_down"]

            def down_rows(layer, quarter):
                return down[layer, bass.ds(quarter * D, D), :]


            with sp.Fori(0, QUARTERS - 1) as j:
                mixed(T_MLP0, up[0], j * D + D, ada[1], j * D, j, 32)
                mixed(T_MLP0 + 16, down_rows(0, j + 1), 0, ada[1], j * D + 3 * D, j, 32)
            unit(T_MLP0_LAST, up[0], 0)
            unit(T_MLP0_LAST + 8, down_rows(0, 0), 0)
            cw = ins["conv_w_in"][0]
            unit(T_CG, cw, D)
            unit(T_XT, cw, 2 * D)
            unit(T_BG, cw, 0)
            unit(T_COUT, ins["conv_w_out"][0], 0)
            with sp.Fori(0, QUARTERS - 1) as j:
                unit(T_MLP1, up[1], j * D + D, j, 16)
                unit(T_MLP1 + 8, down_rows(1, j + 1), 0, j, 16)
            unit(T_MLP1_LAST, up[1], 0)
            unit(T_MLP1_LAST + 8, down_rows(1, 0), 0)
            for m in range(KT):
                sp.wait_ge(s_fo, m + 1)
                nc.sync.dma_start(outs[0][0].rearrange("(j p) n -> p j n", p=P)[:, :, m * P:m * P + P],
                                  yrow[:, :, m * P:m * P + P]).then_inc(s_out, 16)
            nc.sync.dma_start(outs[1].rearrange("(h b) t n -> (b t) h n", h=2), yrow_s[:, :, :]).then_inc(s_out, 16)
            sp.wait_ge(s_out, 16 * N_STORES)

        @block.scalar
        def _(act):
            chain = Count(act, s_a)

            def hi(t, j=None, per=0):
                if t >= T_END:
                    return
                act.wait_ge(s_raw[t % SLOTS], at(16 * (t // SLOTS + 1), j, per // SLOTS * 16))
                if t >= SLOTS:
                    act.wait_ge(s_used, at(t - SLOTS + 1, j, per))
                nc.scalar.activation(wh[:, t % SLOTS], raw[:, t % SLOTS], ACT.Copy).then_inc(s_hi, 1)

            def to_stage(func, free=None, **kw):
                def evac(t, g, j, per_t, per_g):
                    act.wait_ge(s_used, at(t + 1, j, per_t))
                    if g >= 2:
                        act.wait_ge(s_dr, at(g - 1, j, per_g))
                    nc.scalar.activation(halves(stage[g % 2][:, :]), slot(g), func, **kw).then_inc(s_ev, 1)
                return evac

            def to_v(t, g, j, per_t, per_g):
                act.wait_ge(s_used, t + 1)
                act.wait_ge(s_dr, g - 1)
                nc.scalar.activation(vs[g % 2][:, :].rearrange("p (h c) -> p h c", h=2), slot(g)[:, :, PH:HALF], ACT.Copy)
                nc.scalar.activation(halves(stage[g % 2][:, :]), slot(g), ACT.Copy).then_inc(s_ev, 1)

            def to_qk(t, g, j, per_t, per_g):
                m = g - G_QK
                act.wait_ge(s_used, t + 1)
                dst = qT if m < 4 else kT
                nc.scalar.activation(halves(dst[:, m % 4, :]), slot(g), ACT.Copy).then_inc(s_ev, 1)

            def to_u(t, g, j, per_t, per_g):
                m = g - G_CG
                act.wait_ge(s_used, t + 1)
                ps = slot(g)
                nc.scalar.activation(u[:, m, 2:2 + SEQ].rearrange("p (h c) -> p h c", h=2),
                                     ps[:, :, 0:PH], ACT.Copy)
                nc.scalar.activation(
                    u[:, m, 2 + SEQ:UROW].rearrange("p (h b t) -> p h b t", h=2, t=2 + ST)[:, :, :, 2:2 + ST],
                    ps[:, :, PH:HALF].rearrange("p h (b t) -> p h b t", t=ST), ACT.Copy).then_inc(s_ev, 1)

            def ada_pair(t, pair, k, j=None, per_t=0, per_k=0):
                act.wait_ge(s_used, at(t + 2, j, per_t))
                if k >= 4:
                    act.wait_ge(s_tr, at(k // 4, j, per_k // 4))
                nc.scalar.activation(modrow[:, 2 * P * pair:2 * P * (pair + 1)], B4[0:2 * NSEQ, 0:2 * P], ACT.Copy)\
                    .then_inc(s_ae, 1)

            def ada_cols(n, j=None, per=0):
                act.wait_ge(s_tr, at(n + 1, j, per))
                if n >= 1:
                    act.wait_ge(s_cmb, at(n, j, per))
                nc.scalar.activation(modps[:, :, :], B6[:, 0:KT * 2 * NSEQ].rearrange("p (k c) -> p k c", k=KT),
                                     ACT.Copy).then_inc(s_at, 1)

            def unit(t0, g0, evac, j=None, per_t=0, per_g=0):
                for m in range(KT):
                    hi(t0 + m + LEAD, j, per_t)
                    evac(t0 + m, g0 + m, j, per_t, per_g)

            def mixed(t0, g0, n, evac, j=None, per_t=0, per_g=0, per_n=0):
                for m in range(0, KT, 2):
                    t = t0 + 2 * m
                    hi(t + LEAD, j, per_t)
                    hi(t + 1 + LEAD, j, per_t)
                    ada_pair(t, m // 2, 4 * n + m // 2, j, per_t, 4 * per_n)
                    for i in range(2):
                        hi(t + 2 + i + LEAD, j, per_t)
                        evac(t + 2 + i, g0 + m + i, j, per_t, per_g)
                ada_cols(n, j, per_n)

            def norm_root(n):
                act.wait_ge(s_stat, n + 1)
                nc.scalar.activation(rstd[:, 0:HALF], B5[:, 0:HALF], ACT.Sqrt, bias=epsc[:, :], scale=1.0 / D)
                nc.scalar.activation(rstd[:, HALF:TOK], B7[:, 0:HALF], ACT.Sqrt, bias=epsc[:, :], scale=1.0 / D)\
                    .then_inc(s_root, 1)

            def norm_hi(n, x0):
                for k in range(KT):
                    act.wait_ge(s_hh, 8 * n + k + 1)
                    nc.scalar.activation(Xh[:, k, :], hb[k % 2][:, :], ACT.Copy).then_inc(s_hhi, 1)

            nc.scalar.dma_start(crow[0:1, 0, :], ins["c_prompt"]).then_inc(s_cin, 16)
            nc.scalar.dma_start(crow[1:NSEQ, 0, :], ins["c_sample"]).then_inc(s_cin, 16)
            for j in range(NJ):
                nc.scalar.dma_start(xin[:, j, :], ins["x_prompt"][0, j * P:(j + 1) * P, :]).then_inc(s_xin, 16)
            nc.scalar.dma_start(xin[0:NS, NJ, :], ins["x_sample"].rearrange("b t n -> (b t) n")).then_inc(s_xin, 16)
            nc.scalar.dma_start(parrow0[0:96, :], ins["ada_b"].rearrange("l (a p) -> (l a) p", p=P)).then_inc(s_pin, 16)
            nc.scalar.dma_start(parrow0[96:128, :], ins["norm_g"].rearrange("l w (a p) -> (l w a) p", p=P)).then_inc(s_pin, 16)
            nc.scalar.dma_start(parrow1[0:8, :], ins["final_norm_g"].rearrange("(a p) -> a p", p=P)).then_inc(s_pin, 16)
            nc.scalar.dma_start(parrow1[8:16, :], ins["mlstm_head_g"].rearrange("l (a p) -> (l a) p", p=P)).then_inc(s_pin, 16)
            nc.scalar.dma_start(parrow1[16:40, :], ins["conv_w"].rearrange("l w (a p) -> (l w a) p", p=P)).then_inc(s_pin, 16)
            act.wait_ge(s_cin, 32)
            nc.scalar.activation(crow[:, 1, :], crow[:, 0, :], ACT.Exp, scale=-1.0).then_inc(s_silu, 1)
            for t in range(LEAD + 1):
                hi(t)
            for k in range(KT):
                act.wait_ge(s_xt, k + 1)
                nc.scalar.activation(prompt(xT[:, k, :]), G[:, k % 4, :].rearrange("p (h c) -> p h c", h=2), ACT.Copy)\
                    .then_inc(s_xe, 1)
            for t0 in (T_ADA0, T_ADA1):
                for m in range(0, KT, 2):
                    t = t0 + m
                    if t:
                        hi(t + LEAD)
                    hi(t + 1 + LEAD)
                    ada_pair(t, m // 2, t // 2)
                ada_cols(t0 // 8)
            act.wait_ge(s_gin, 80)
            nc.scalar.activation(gh[:, :, :], graw[:, :, :], ACT.Copy).then_inc(s_gs, 1)
            norm_root(0)
            norm_hi(0, X_NORM0)
            act.wait_ge(s_xse, 1)
            nc.scalar.dma_start(xspill, xT[:, :, :].rearrange("p k c -> p (k c)")).then_inc(s_spill, 16)
            act.wait_ge(s_rv, 1)
            chain.link(nc.scalar.activation(rows[1][:, :], rows[0][:, :], ACT.Exp, scale=-1.0))
            nc.scalar.activation(rows[2][:, :], rows[1][:, :], ACT.Ln, bias=1.0).then_inc(s_ra, 1)
            act.wait_ge(s_rv, 2)
            nc.scalar.activation(rows[5][:, :], rows[0][:, :], ACT.Exp, scale=-1.0).then_inc(s_ra, 1)
            for hf in range(2):
                nc.scalar.activation(rows[1][:, hf * HALF:hf * HALF + PH], rows[3][:, hf * HALF:hf * HALF + PH],
                                     ACT.Exp, bias=rows[4][:, LAST_COL:LAST_COL + 1])
            act.wait_ge(s_rv, 3)
            nc.scalar.activation(sample(rows[1][:, :]), sample(rows[1][:, :]), ACT.Exp)
            nc.scalar.activation(sample(rows[2][:, :]), sample(rows[2][:, :]), ACT.Exp).then_inc(s_ra, 1)
            act.wait_ge(s_ra, 3)
            for i, r in enumerate((3, 1, 5, 4, 2)):
                nc.scalar.dma_start(bounce[i].rearrange("h (a c) -> h a c", a=2), sample(rows[r][:, :])).then_inc(s_bo, 16)
            nc.scalar.dma_start(outs[4][0, 0, :].rearrange("(h o) -> h o", o=1), rows[0][:, LAST_COL:LAST_COL + 1]).then_inc(s_bo, 16)
            for hf in range(2):
                nc.scalar.dma_start(outs[8][0, 4 * hf:4 * hf + 4].rearrange("b h -> h b"),
                                    sample4(rows[0][:, :])[:, hf, :, ST - 1]).then_inc(s_bo, 16)
            act.wait_ge(s_bo, 16 * 8)
            by_token = lambda i: bounce[i].rearrange("h s -> s h")
            nc.scalar.dma_start(g_s[:, :], by_token(0)).then_inc(s_bi, 16)
            nc.scalar.dma_start(a_s[:, :], by_token(1)).then_inc(s_bi, 16)
            act.wait_ge(s_spill, 16)
            act.wait_ge(s_kx, X_NORM0 + 8)
            nc.scalar.dma_start(negM_s[:, :, :], bounce[3:4].rearrange("o h s -> o (h s)").broadcast_to((NS, H * NS))
                                .rearrange("p (h s) -> p h s", h=H)).then_inc(s_bi, 16)
            for h2 in range(2):
                pair = bounce[2].rearrange("(a h) s -> h s a", h=2)
                nc.scalar.dma_start(enm_s[NS * h2:NS * (h2 + 1), :], pair[h2]).then_inc(s_bi, 16)
                pair = bounce[4:5].rearrange("o (a h) s -> h o a s", h=2)
                nc.scalar.dma_start(einter_s[DK * h2:DK * (h2 + 1), :, :],
                                    pair[h2].broadcast_to((DK, H // 2, NS))).then_inc(s_bi, 16)
            mixed(T_QK, G_QK, 2, to_qk)
            act.wait_ge(s_xst, 1)
            for h2 in range(2):
                for b in range(SB):
                    nc.scalar.dma_start(C0[DK * h2:DK * (h2 + 1), b, :, 0:DV],
                                        ins["state_mlstm_C"][0, b].rearrange("(a h) d e -> h d a e", h=2)[h2]).then_inc(s_sin, 16)
                nc.scalar.dma_start(C0[DK * h2:DK * (h2 + 1), :, :, DV:DVA].rearrange("p b a o -> p (b a) o"),
                                    ins["state_mlstm_n"][0].rearrange("b (a h) d -> h d (b a)", h=2)[h2]
                                    .rearrange("d (b o) -> d b o", o=1)).then_inc(s_sin, 16)
            mixed(T_V, G_V, 3, to_v)
            act.wait_ge(s_sp, 1)
            nc.scalar.activation(dec_s[:, :, :], dec_s[:, :, :], ACT.Exp).then_inc(s_sd, 1)
            mixed(T_O, G_O, 4, to_stage(ACT.Exp, scale=-1.0))
            act.wait_ge(s_spv, 1)
            for a in range(H // 2):
                last = nc.scalar.activation(num_s[:, a, :], G[0:2 * NS, a, 0:DVA], ACT.Copy)
            last.then_inc(s_snum, 1)
            act.wait_ge(s_cud, 1)
            for h2 in range(2):
                for b in range(SB):
                    nc.scalar.dma_start(outs[6][0, b].rearrange("(a h) d e -> h d a e", h=2)[h2],
                                        C0[DK * h2:DK * (h2 + 1), b, :, 0:DV]).then_inc(s_out, 16)
                nc.scalar.dma_start(outs[7][0].rearrange("b (a h) d -> h d (b a)", h=2)[h2].rearrange("d (b o) -> d b o", o=1),
                                    C0[DK * h2:DK * (h2 + 1), :, :, DV:DVA].rearrange("p b a o -> p (b a) o")).then_inc(s_out, 16)
            for h in range(H + 1):
                if h < H:
                    act.wait_ge(s_bc, h + 1)
                    if h >= 2:
                        act.wait_ge(s_pv, h - 1)
                    o = 0
                    for i in range(NJ):
                        w = SEQ - P * i
                        nc.scalar.activation(probs[h % 2][:, o:o + w], B4[:, P * i:SEQ], ACT.Exp,
                                             bias=tok[:, 0, i, h:h + 1]).then_inc(s_d, 1)
                        o += w
                if h >= 1:
                    act.wait_ge(s_pv, h)
                    if h >= 3:
                        act.wait_ge(s_hs, h - 2)
                    for half in range(2):
                        last = nc.scalar.activation(num[(h - 1) % 2][:, 2 * half:2 * half + 2, :],
                                                    (B6, B7)[half][:, 0:2 * DVA].rearrange("p (j e) -> p j e", j=2), ACT.Copy)
                    last.then_inc(s_num, 1)
            act.wait_ge(s_cp, 1)
            for b in range(3):
                n = min(3, H - 3 * b)
                last = nc.scalar.activation(Cp[:, 3 * b:3 * b + n, :],
                                            G[0:DK, b, 0:n * DVA].rearrange("p (h e) -> p h e", h=n), ACT.Copy)
            last.then_inc(s_cpo, 1)
            act.wait_ge(s_cpo, 1)
            nc.scalar.dma_start(outs[2][0, 0].rearrange("h d e -> d h e"), Cp[:, :, 0:DV]).then_inc(s_out, 16)
            nc.scalar.dma_start(outs[3][0, 0].rearrange("h (d o) -> d h o", o=1), Cp[:, :, DV:DVA]).then_inc(s_out, 16)
            act.wait_ge(s_y, H)
            act.wait_ge(s_num, H)
            for k in range(KT):
                nc.scalar.dma_start(xT[:, k, :], xspill[:, k * TOK:(k + 1) * TOK]).then_inc(s_back, 16)
            mixed(T_WOUT, G_WOUT, 5, to_stage(ACT.Copy))
            norm_root(1)
            norm_hi(1, X_NORM1)
            with act.Fori(0, QUARTERS - 1) as j:
                mixed(T_MLP0, G_MLP0, 6, to_stage(ACT.Relu), j, 32, 16, 2)
                mixed(T_MLP0 + 16, G_MLP0 + 8, 7, to_stage(ACT.Copy), j, 32, 16, 2)
            unit(T_MLP0_LAST, G_MLP0_LAST, to_stage(ACT.Relu))
            nc.scalar.dma_start(crows[:, :], ins["state_conv"][0].rearrange("b r n -> (b r) n")).then_inc(s_crin, 16)
            unit(T_MLP0_LAST + 8, G_MLP0_LAST + 8, to_stage(ACT.Copy))
            norm_root(2)
            norm_hi(2, X_NORM2)
            act.wait_ge(s_crt, 1)
            nc.scalar.activation(
                u[:, :, 2 + SEQ:UROW].rearrange("p k (b t) -> p k b t", t=2 + ST)[:, :, :, 0:2],
                B6[:, 0:KT * 2 * SB].rearrange("p (k b r) -> p k b r", k=KT, r=2), ACT.Copy).then_inc(s_cre, 1)
            unit(T_CG, G_CG, to_u)
            unit(T_XT, G_XT, to_stage(ACT.Copy))
            unit(T_BG, G_BG, to_stage(ACT.Copy))
            act.wait_ge(s_ult, 1)
            for i, bank in enumerate((B4, B6)):
                last = nc.scalar.activation(urows[:, i * 512:(i + 1) * 512], bank[0:2 * NSEQ, :], ACT.Copy)
            last.then_inc(s_ulo, 1)
            act.wait_ge(s_ulo, 1)
            nc.scalar.dma_start(outs[5][0, 0], urows[0:2, :]).then_inc(s_out, 16)
            nc.scalar.dma_start(outs[9][0].rearrange("b r n -> (b r) n"), urows[2:2 * NSEQ, :]).then_inc(s_out, 16)
            unit(T_COUT, G_COUT, to_stage(ACT.Copy))
            norm_root(3)
            norm_hi(3, X_NORM3)
            with act.Fori(0, QUARTERS - 1) as j:
                unit(T_MLP1, G_MLP1, to_stage(ACT.Relu), j, 16, 16)
                unit(T_MLP1 + 8, G_MLP1 + 8, to_stage(ACT.Copy), j, 16, 16)
            unit(T_MLP1_LAST, G_MLP1_LAST, to_stage(ACT.Relu))
            unit(T_MLP1_LAST + 8, G_MLP1_LAST + 8, to_stage(ACT.Copy))
            norm_root(4)
            for m in range(KT):
                act.wait_ge(s_ft, m + 1)
                nc.scalar.activation(yrow[:, :, m * P:m * P + P], G[:, m % 4, :].rearrange("p (j c) -> p j c", j=NJ), ACT.Copy)
                nc.scalar.activation(yrow_s[:, :, m * P:m * P + P],
                                     (B4, B6)[m % 2][0:SH, 0:2 * P].rearrange("p (j c) -> p j c", j=2), ACT.Copy).then_inc(s_fo, 1)

        @block.gpsimd
        def _(pool):
            chain = Count(pool, s_p)

            def lo(t, j=None, per=0):
                if t >= T_END:
                    return
                pool.wait_ge(s_hi, at(t + 1, j, per))
                nc.gpsimd.tensor_tensor(wl[:, t % SLOTS], raw[:, t % SLOTS], wh[:, t % SLOTS].bitcast(F32),
                                        ALU.subtract).then_inc(s_lo[t % 2], 1)

            def lows(t0, t1, j=None, per=0):
                for t in range(t0, t1):
                    lo(t, j, per)

            def norm_lo(n):
                for k in range(KT):
                    pool.wait_ge(s_hhi, 8 * n + k + 1)
                    nc.gpsimd.tensor_tensor(Xl[:, k, :], hb[k % 2][:, :], Xh[:, k, :].bitcast(F32), ALU.subtract)\
                        .then_inc(s_kx, 1)

            chain.link(nc.gpsimd.memset(ident[:, :], 0.0))
            nc.gpsimd.affine_select(out=ident[:, :], in_=ident[:, :], compare_op=ALU.not_equal, fill=1.0, base=0,
                                    pattern=[[-1, P]], channel_multiplier=1)
            nc.gpsimd.memset(epsc[:, :], EPS)
            nc.gpsimd.memset(mhalf[:, :], -0.5)
            nc.gpsimd.memset(ones[:, :], 1.0)
            chain.link(nc.gpsimd.memset(mask_b[:, :], 1.0))
            chain.link(nc.gpsimd.affine_select(out=mask_b[:, :], in_=mask_b[:, :], compare_op=ALU.is_ge, fill=0.0, base=0,
                                               pattern=[[-ST, SB]], channel_multiplier=1))
            chain.link(nc.gpsimd.affine_select(out=mask_b[:, :], in_=mask_b[:, :], compare_op=ALU.is_ge, fill=0.0, base=ST - 1,
                                               pattern=[[ST, SB]], channel_multiplier=-1))
            nc.gpsimd.memset(graw[:, :, :], 0.0).then_inc(s_const, 1)
            pool.wait_ge(s_const, 1)
            gates = ins["mlstm_w_in"][0].rearrange("(k p) n -> p k n", p=P)[:, :, 3 * D:3 * D + 2 * H]
            nc.gpsimd.dma_start(graw[:, :, 0:H], gates[:, :, 0:H]).then_inc(s_gin, 16)
            nc.gpsimd.dma_start(graw[:, :, 32:32 + H], gates[:, :, H:2 * H]).then_inc(s_gin, 16)
            bg = ins["mlstm_b_gates"].rearrange("o (g h) -> g h o", g=2)
            nc.gpsimd.dma_start(bgate[0:H, :], bg[0]).then_inc(s_gin, 16)
            nc.gpsimd.dma_start(bgate[32:32 + H, :], bg[1]).then_inc(s_gin, 16)
            nc.gpsimd.dma_start(m0row[:, :], ins["state_mlstm_m"][0].rearrange("b h -> h b")).then_inc(s_gin, 16)
            for t in range(T_ADA0 + 1, T_QK, 2):
                lo(t)
            for t in range(T_QK, T_QK + LEAD):
                pool.wait_ge(s_lo[0], T_QK // 2)
                lo(t)
            norm_lo(0)
            lows(T_QK + LEAD, T_V)
            pool.wait_ge(s_bi, 16 * 7)
            nc.gpsimd.memset(probs_s[:, :, :], 0.0)
            nc.gpsimd.memset(qbd[:, :, :, :], 0.0).then_inc(s_srs, 1)
            nc.gpsimd.memset(vtok_s[:, :, DV:DVA], 1.0)
            lows(T_V, T_O)
            pool.wait_ge(s_sd, 1)
            dv = dec_s[:, :, :].rearrange("p h (b t) -> p h b t", t=ST)
            masks = 0
            for pattern, b0, cm in (([[0, H], [-ST, SB], [0, ST]], 0, 1),
                                    ([[0, H], [ST, SB], [0, ST]], ST - 1, -1),
                                    ([[0, H], [ST, SB], [1, ST]], 0, -1)):
                nc.gpsimd.affine_select(out=dv, in_=dv, compare_op=ALU.is_ge, fill=0.0, base=b0, pattern=pattern,
                                        channel_multiplier=cm).then_inc(s_srs, 1)
                masks += 1
                pool.wait_ge(s_srs, 1 + masks)
            lows(T_O, T_WOUT)
            pool.wait_ge(s_tr, 5)
            chain.link(nc.gpsimd.memset(sel[:, :, :], 0.0))
            nc.gpsimd.affine_select(out=sel[:, :, :], in_=sel[:, :, :], compare_op=ALU.not_equal, fill=1.0, base=0,
                                    pattern=[[-1, H], [0, P]], channel_multiplier=1).then_inc(s_selr, 1)
            lows(T_WOUT, T_WOUT + LEAD)
            pool.wait_ge(s_sp, 4)
            nc.gpsimd.tensor_tensor(stat[0:2 * NS, 3, :], stat[0:2 * NS, 2, :], mhalf[0:2 * NS, :], ALU.pow).then_inc(s_rs, 1)
            for h in range(H + 2):
                if h < H:
                    o = 0
                    for i in range(NJ):
                        pool.wait_ge(s_d, NJ * h + i + 1)
                        diag = probs[h % 2][:, o:o + P]
                        nc.gpsimd.affine_select(out=diag, in_=diag, compare_op=ALU.is_ge, fill=0.0, base=0,
                                                pattern=[[1, P]], channel_multiplier=-1).then_inc(s_sel, 1)
                        o += SEQ - P * i
                if 1 <= h <= H:
                    pool.wait_ge(s_sq, h)
                    nc.gpsimd.tensor_tensor(stat[:, 3, :], stat[:, 2, :], mhalf[:, :], ALU.pow).then_inc(s_rs, 1)
                if h >= 2:
                    g = h - 2
                    pool.wait_ge(s_yh, g + 1)
                    nc.gpsimd.tensor_tensor(Xl[:, g, :], og[:, g, :], Xh[:, g, :].bitcast(F32), ALU.subtract)\
                        .then_inc(s_kx, 1)
            lows(T_WOUT + LEAD, T_MLP0 + LEAD)
            norm_lo(1)
            with pool.Fori(0, QUARTERS - 1) as j:
                lows(T_MLP0 + LEAD, T_MLP0 + LEAD + 32, j, 32)
            lows(T_MLP0_LAST + LEAD, T_CG + LEAD)
            norm_lo(2)
            nc.gpsimd.memset(u[:, :, 0:2], 0.0).then_inc(s_cre, 1)
            lows(T_CG + LEAD, T_MLP1 + LEAD)
            norm_lo(3)
            with pool.Fori(0, QUARTERS - 1) as j:
                lows(T_MLP1 + LEAD, T_MLP1 + LEAD + 16, j, 16)
            lows(T_MLP1_LAST + LEAD, T_END)

        @block.vector
        def _(dve):
            chain = Count(dve, s_v)
            V = nc.vector
            mids = {"n": 0}

            def mid(ins_, j=None, per=0):
                ins_.then_inc(s_mid, 1)
                mids["n"] += 1
                dve.wait_ge(s_mid, at(mids["n"], j, per))

            def drain_square(hi_out, lo_out, other):
                def drain(m, g, j, per):
                    dve.wait_ge(s_ev, at(g + 1, j, per))
                    dve.wait_ge(s_dr, at(g, j, per))
                    s = stage[g % 2][:, :]
                    o = s if other is None else other[:, m, :]
                    V.tensor_tensor(hi_out[:, m, :], s, o, ALU.mult)
                    mid(V.tensor_tensor(sqb[:, :], s, o, ALU.mult), j, per)
                    V.tensor_tensor(lo_out[:, m, :], sqb[:, :], hi_out[:, m, :].bitcast(F32), ALU.subtract)\
                        .then_inc(s_dr, 1)
                return drain

            def residual(gate, stats_before=None):
                def drain(m, g, j, per):
                    dve.wait_ge(s_ev, at(g + 1, j, per))
                    dve.wait_ge(s_dr, at(g, j, per))
                    s = stage[g % 2][:, :]
                    gt = modT[:, gate, m, :]
                    V.scalar_tensor_tensor(prompt(xT[:, m, :]), prompt(s), gt[:, 0:1], prompt(xT[:, m, :]),
                                           ALU.mult, ALU.add)
                    mid(V.tensor_tensor(
                        small_s[:, :].rearrange("p (h b t) -> p h b t", h=2, t=ST), sample4(s),
                        gt[:, 1:NSEQ].rearrange("p (h b) -> p h b", h=2).unsqueeze(3).broadcast_to((P, 2, ST, ST)),
                        ALU.mult), j, per)
                    V.tensor_tensor(sample(xT[:, m, :]), sample(xT[:, m, :]),
                                    small_s[:, :].rearrange("p (h c) -> p h c", h=2), ALU.add).then_inc(s_dr, 1)
                    if stats_before is not None:
                        dve.wait_ge(s_dr, g + 1)
                        squares(m, stats_before)
                return drain

            def squares(m, n):
                if m == 0:
                    if n >= 1:
                        dve.wait_ge(s_kx, (X_NORM0, X_NORM1, X_NORM2, X_NORM3)[n - 1] + KT)
                    chain.link(V.tensor_tensor(acc[:, :], xT[:, m, :], xT[:, m, :], ALU.mult))
                else:
                    chain.link(V.tensor_tensor(sqb[:, :], xT[:, m, :], xT[:, m, :], ALU.mult))
                    ins_ = V.tensor_tensor(acc[:, :], acc[:, :], sqb[:, :], ALU.add)
                    if m == KT - 1:
                        ins_.then_inc(s_acc, 1)
                    else:
                        chain.link(ins_)

            def unit(g0, drain, j=None, per=0):
                for m in range(KT):
                    drain(m, g0 + m, j, per)

            def combine(n, dst, bias_col, j=None, per=0):
                dve.wait_ge(s_at, at(n + 1, j, per))
                if n >= 1:
                    dve.wait_ge(s_mod, at(n, j, per))
                V.tensor_tensor(modsum[:, :, :], modps[:, :, 0:NSEQ], modps[:, :, NSEQ:2 * NSEQ], ALU.add)\
                    .then_inc(s_cmb, 1)
                dve.wait_ge(s_cmb, at(n + 1, j, per))
                V.tensor_tensor(modT[:, dst, :, :], modsum[:, :, :],
                                par0[:, bass.ds(bias_col, KT)].unsqueeze(2).broadcast_to((P, KT, NSEQ)), ALU.add)\
                    .then_inc(s_mod, 1)

            def norm_apply(n, layer, which):
                sc, sh = layer * NMOD + 3 * which + 1, layer * NMOD + 3 * which
                dve.wait_ge(s_mod, (2, 5, 12, 12)[n])
                if n >= 1:
                    dve.wait_ge(s_hh, KT * n)
                chain.link(V.tensor_scalar(gain[:, :, :], modT[:, sc, :, :], 1.0, None, ALU.add))
                gcol = 96 + (layer * 2 + which) * KT
                chain.link(V.tensor_tensor(gain[:, :, :], gain[:, :, :],
                                           par0[:, gcol:gcol + KT].unsqueeze(2).broadcast_to((P, KT, NSEQ)), ALU.mult))
                dve.wait_ge(s_root, n + 1)
                chain.link(V.reciprocal(rstd[:, :], rstd[:, :]))
                for k in range(KT):
                    hk = hb[k % 2]
                    if k >= 2:
                        dve.wait_ge(s_kx, (X_NORM0, X_NORM1, X_NORM2, X_NORM3)[n] + k - 1)
                    chain.link(V.tensor_tensor(xr[:, :], xT[:, k, :], rstd[:, :], ALU.mult))
                    if n + k >= 1:
                        dve.wait_ge(s_hh, KT * n + k)
                    V.tensor_scalar(prompt(hk[:, :]), prompt(xr[:, :]), gain[:, k, 0:1], modT[:, sh, k, 0:1],
                                    ALU.mult, ALU.add)
                    seqs = lambda t: t[:, k, 1:NSEQ].rearrange("p (h b) -> p h b", h=2).unsqueeze(3)\
                        .broadcast_to((P, 2, ST, ST))
                    chain.link(V.tensor_tensor(small_s[:, :].rearrange("p (h b t) -> p h b t", h=2, t=ST),
                                               sample4(xr[:, :]), seqs(gain), ALU.mult))
                    V.tensor_tensor(sample4(hk[:, :]), small_s[:, :].rearrange("p (h b t) -> p h b t", h=2, t=ST),
                                    seqs(modT[:, sh]), ALU.add).then_inc(s_hh, 1)

            dve.wait_ge(s_silu, 1)
            chain.link(V.tensor_scalar(crow[:, 1, :], crow[:, 1, :], 1.0, None, ALU.add))
            chain.link(V.reciprocal(crow[:, 2, :], crow[:, 1, :]))
            V.tensor_tensor(crow[:, 1, :], crow[:, 0, :], crow[:, 2, :], ALU.mult).then_inc(s_silu, 1)
            dve.wait_ge(s_ct, 1)
            chain.link(V.tensor_copy(ccol[:, :, :], B5[:, 0:KT * NSEQ].rearrange("p (k c) -> p k c", k=KT)))
            chain.link(V.tensor_copy(c2[:, :, 0:NSEQ], ccol[:, :, :]))
            V.tensor_tensor(c2[:, :, NSEQ:2 * NSEQ], ccol[:, :, :], c2[:, :, 0:NSEQ].bitcast(F32), ALU.subtract)\
                .then_inc(s_cs, 1)
            dve.wait_ge(s_pt, 1)
            V.tensor_copy(par0[:, :], B7[:, 0:P])
            V.tensor_copy(par1[:, :], B7[:, P:P + 40]).then_inc(s_ptd, 1)
            dve.wait_ge(s_ptd, 1)
            dve.wait_ge(s_xst, 1)
            for k in range(KT):
                last = V.tensor_copy(sample(xT[:, k, :]), B6[:, NS * k:NS * (k + 1)].rearrange("p (h c) -> p h c", h=2))
            last.then_inc(s_xse, 1)
            dve.wait_ge(s_xse, 1)
            for n, t0 in enumerate((T_ADA0, T_ADA1)):
                for t in range(t0, t0 + KT, 2):
                    dve.wait_ge(s_hi, t + 1)
                    V.tensor_tensor(wl[:, t % SLOTS], raw[:, t % SLOTS], wh[:, t % SLOTS].bitcast(F32), ALU.subtract)\
                        .then_inc(s_lo[0], 1)
                    if n == 0 and t >= 2:
                        for k in (t - 2, t - 1):
                            dve.wait_ge(s_xe, k + 1)
                            squares(k, 0)
                if n == 0:
                    for k in (6, 7):
                        dve.wait_ge(s_xe, k + 1)
                        squares(k, 0)
                combine(n, n, n * KT)
            dve.wait_ge(s_gs, 1)
            V.tensor_tensor(gl[:, :, :], graw[:, :, :], gh[:, :, :].bitcast(F32), ALU.subtract).then_inc(s_gs, 1)
            norm_apply(0, 0, 0)
            dve.wait_ge(s_gp, 1)
            dve.wait_ge(s_gin, 80)
            R = [r[:, :] for r in rows]
            lf = sqb[0:H, :]
            for hf, bank in enumerate((B5, B7)):
                cols = slice(hf * HALF, (hf + 1) * HALF)
                V.tensor_scalar(R[3][:, cols], bank[0:H, 0:HALF], bgate[0:H, :], None, ALU.add)
                V.tensor_scalar(R[4][:, cols], bank[32:32 + H, 0:HALF], bgate[32:32 + H, :], None, ALU.add)
            chain.link(V.memset(xr[0:H, :], 1.0))
            V.scalar_tensor_tensor(R[0], R[4], -1.0, R[4], ALU.mult, ALU.max).then_inc(s_rv, 1)
            dve.wait_ge(s_ra, 1)
            chain.link(V.scalar_tensor_tensor(lf, R[4], 0.0, R[2], ALU.min, ALU.subtract))
            chain.link(V.tensor_tensor_scan(R[1][:, 0:PH], xr[0:H, 0:PH], lf[:, 0:PH], 0.0, ALU.mult, ALU.add))
            chain.link(V.tensor_tensor_scan(R[1][:, HALF:HALF + PH], xr[0:H, 0:PH], lf[:, HALF:HALF + PH],
                                            R[1][:, PH - 1:PH], ALU.mult, ALU.add))
            S4 = [sample4(r) for r in R]
            chain.link(V.tensor_copy(S4[1][:, :, :, 0], sample4(lf)[:, :, :, 0]))
            for t in range(1, ST):
                chain.link(V.tensor_tensor(S4[1][:, :, :, t], S4[1][:, :, :, t - 1], sample4(lf)[:, :, :, t], ALU.add))
            chain.link(V.tensor_tensor(R[3], R[3], R[1], ALU.subtract))
            chain.link(V.tensor_tensor_scan(R[2][:, 0:PH], xr[0:H, 0:PH], R[3][:, 0:PH], 0.0, ALU.mult, ALU.max))
            chain.link(V.tensor_tensor_scan(R[2][:, HALF:HALF + PH], xr[0:H, 0:PH], R[3][:, HALF:HALF + PH],
                                            R[2][:, PH - 1:PH], ALU.mult, ALU.max))
            m0 = m0row[:, :].rearrange("h (a b) -> h a b", a=2)
            for t in range(ST):
                chain.link(V.tensor_tensor(S4[2][:, :, :, t], S4[2][:, :, :, t - 1] if t else m0, S4[3][:, :, :, t], ALU.max))
            V.tensor_tensor(R[0], R[1], R[2], ALU.add)
            V.tensor_scalar(R[4], R[2], -1.0, None, ALU.mult).then_inc(s_rv, 1)
            dve.wait_ge(s_rv, 2)
            spread = lambda ap: ap.unsqueeze(3).broadcast_to((H, 2, ST, ST))
            dve.wait_ge(s_ra, 2)
            V.tensor_tensor(S4[1], S4[3], spread(S4[4][:, :, :, ST - 1]), ALU.add)
            V.tensor_tensor(S4[2], S4[4], spread(m0), ALU.add)
            dve.wait_ge(s_kx, X_NORM0 + KT)
            V.tensor_copy(negMp[:, :].rearrange("h (a c) -> h a c", a=2), prompt(R[4])).then_inc(s_rv, 1)
            V.memset(vtok[:, :, :, DV:DVA], 1.0)
            nvt = {"n": 0}

            def turned(dst, dst_s):
                nvt["n"] += 1
                dve.wait_ge(s_vt, nvt["n"])
                V.tensor_copy(dst, B7[:, :].rearrange("p (j c) -> p j c", j=NJ))
                V.tensor_copy(dst_s, B5[0:NS, 0:P]).then_inc(s_vtd, 1)

            dve.wait_ge(s_ra, 3)
            dve.wait_ge(s_tt, 1)
            V.tensor_copy(tok[:, :, :, :], B7[:, 0:3 * NJ * H].rearrange("p (a j h) -> p a j h", a=3, j=NJ)).then_inc(s_ttd, 1)
            dve.wait_ge(s_spill, 16)
            for m in range(KT):
                g = G_QK + m
                dve.wait_ge(s_ev, g + 1)
                src, dst = (qT, qs) if m < 4 else (kT, ks)
                V.tensor_copy(dst[:, m % 4, :].rearrange("p (h c) -> p h c", h=2), sample(src[:, m % 4, :])).then_inc(s_dr, 1)
                if m >= 5:
                    n = m - 5
                    turned(ktok[:, :, n * P:(n + 1) * P], ktok_s[:, n * P:(n + 1) * P])
            turned(ktok[:, :, 3 * P:4 * P], ktok_s[:, 3 * P:4 * P])
            combine(2, 2, 2 * KT)
            for m in range(KT):
                nvt["n"] += 1
                dve.wait_ge(s_vt, nvt["n"])
                V.tensor_copy(vtok[:, :, m, 0:DV], B7[:, :].rearrange("p (j c) -> p j c", j=NJ))
                V.tensor_copy(vtok_s[:, m, 0:DV], B5[0:NS, 0:P]).then_inc(s_dr, 1)
            combine(3, 3, 3 * KT)
            dve.wait_ge(s_dr, G_O)
            KS = DK ** -0.5
            chain.link(V.tensor_scalar(tok[:, 1, :, :], tok[:, 1, :, :], KS, None, ALU.mult))
            dve.wait_ge(s_bi, 16 * 7)
            chain.link(V.tensor_scalar(a_s[:, :], a_s[:, :], KS, None, ALU.mult))
            for jt in range(NJ):
                kv = ktok[:, jt, :].rearrange("p (h d) -> p h d", h=H)
                V.tensor_tensor(kv, kv, tok[:, 1, jt, :].unsqueeze(2).broadcast_to((P, H, DK)), ALU.mult)
            kv = ktok_s[:, :].rearrange("p (h d) -> p h d", h=H)
            chain.link(V.tensor_tensor(kv, kv, a_s[:, :].unsqueeze(2).broadcast_to((NS, H, DK)), ALU.mult))
            chain.link(V.tensor_tensor(dec_s[:, :, :], negM_s[:, :, :], g_s[:, :].unsqueeze(2).broadcast_to((NS, H, NS)), ALU.add))
            V.tensor_scalar(dec_s[:, :, :], dec_s[:, :, :], 0.0, None, ALU.min).then_inc(s_sp, 1)
            dve.wait_ge(s_srs, 1)
            qe = small_s
            chain.link(V.tensor_tensor(sqb[:, 0:H // 2 * NS].rearrange("p (a t) -> p a t", a=H // 2), qs[:, :, :], einter_s[:, :, :], ALU.mult))
            qe = sqb[:, 0:H // 2 * NS].rearrange("p (a t) -> p a t", a=H // 2)
            for h2 in range(2):
                pr = slice(DK * h2, DK * (h2 + 1))
                for b in range(SB):
                    last = V.tensor_copy(qbd[pr, :, b, NS * h2 + ST * b:NS * h2 + ST * (b + 1)], qe[pr, :, ST * b:ST * (b + 1)])
            last.then_inc(s_sp, 1)
            for m in range(KT):
                g = G_O + m
                dve.wait_ge(s_ev, g + 1)
                s = stage[g % 2][:, :]
                chain.link(V.tensor_scalar(s, s, 1.0, None, ALU.add))
                chain.link(V.reciprocal(sqb[:, :], s))
                V.tensor_scalar(og[:, m, :], sqb[:, :], par1[:, 8 + m:9 + m], None, ALU.mult).then_inc(s_dr, 1)
            combine(4, 4, 4 * KT)
            dve.wait_ge(s_ssc, 1)
            dve.wait_ge(s_srs, 4)
            for h2 in range(2):
                pick = lambda ap: ap.rearrange("p (a h) t -> p a h t", h=2)[:, :, h2, :]
                last = V.scalar_tensor_tensor(
                    pick(probs_s[:, :, :])[:, :, NS * h2:NS * (h2 + 1)],
                    (B7, B6)[h2][0:NS, 0:H // 2 * NS].rearrange("p (a t) -> p a t", t=NS), KS,
                    pick(dec_s[:, :, :]), ALU.mult, ALU.mult)
            last.then_inc(s_sp, 1)

            def head_norm(nm, npart, enm, w, sq_sem, rs_n, hs_out, out_sem):
                st = [stat[0:npart, i, 0:w] for i in range(6)]
                den = nm[:, :, DV]
                chain.link(V.scalar_tensor_tensor(st[0], den, -1.0, den, ALU.mult, ALU.max))
                chain.link(V.tensor_tensor(st[0], st[0], enm, ALU.max))
                chain.link(V.reciprocal(st[1], st[0]))
                chain.link(V.tensor_tensor(hs_out, nm[:, :, 0:DV], st[1].unsqueeze(2).broadcast_to((npart, w, DV)), ALU.mult))
                sq = stage[0][0:npart, 0:w * DV].rearrange("p (j e) -> p j e", j=w)
                chain.link(V.tensor_tensor(sq, hs_out, hs_out, ALU.mult))
                chain.link(V.tensor_reduce(st[4], sq, AX.X, ALU.add))
                V.tensor_scalar(st[2], st[4], 1.0 / DV, EPS, ALU.mult, ALU.add).then_inc(sq_sem, 1)
                dve.wait_ge(s_rs, rs_n)
                V.tensor_tensor(hs_out, hs_out, st[3].unsqueeze(2).broadcast_to((npart, w, DV)), ALU.mult).then_inc(out_sem, 1)

            dve.wait_ge(s_snum, 1)
            head_norm(num_s[:, :, :], 2 * NS, enm_s[:, :], H // 2, s_sp, 1, hs[0:2 * NS, :, :], s_sp)
            for a in range(H // 2):
                if a:
                    dve.wait_ge(s_cu, SB * a)
                V.tensor_tensor(kam[:, :, :], ktok_s[:, a * P:(a + 1) * P].unsqueeze(1).broadcast_to((NS, SB, P)),
                                mask_b[:, :].unsqueeze(2).broadcast_to((NS, SB, P)), ALU.mult).then_inc(s_kam, 1)
                for b in range(SB):
                    n = SB * a + b
                    dve.wait_ge(s_cu, n + 1)
                    bank = (B4, B5)[n % 2]
                    for h2 in range(2):
                        pr = slice(DK * h2, DK * (h2 + 1))
                        last = V.scalar_tensor_tensor(C0[pr, b, a, :], C0[pr, b, a, :],
                                                      einter_s[pr, a, ST * b + ST - 1:ST * b + ST],
                                                      bank[pr, h2 * DVA:(h2 + 1) * DVA], ALU.mult, ALU.add)
                    last.then_inc(s_cud, 1) if n == SB * H // 2 - 1 else last.then_inc(s_kam, 1)
            dve.wait_ge(s_sht, 1)
            V.tensor_tensor(og[:, :, :].rearrange("p k (h c) -> p k h c", h=2)[:, :, :, PH:HALF],
                            og[:, :, :].rearrange("p k (h c) -> p k h c", h=2)[:, :, :, PH:HALF],
                            B6[:, 0:H * NS].rearrange("p (k h c) -> p k h c", k=H, h=2), ALU.mult).then_inc(s_sp, 1)
            for h in range(H + 2):
                if h < H:
                    o = 0
                    for i in range(NJ):
                        w = SEQ - P * i
                        dve.wait_ge(s_s, NJ * h + i + 1)
                        dve.wait_ge(s_sel, NJ * h + i + 1)
                        pr = probs[h % 2][:, o:o + w]
                        V.scalar_tensor_tensor(pr, G[:, i, 0:w], KS, pr, ALU.mult, ALU.mult).then_inc(s_pr, 1)
                        o += w
                if 1 <= h <= H:
                    g = h - 1
                    dve.wait_ge(s_num, g + 1)
                    if g:
                        dve.wait_ge(s_ht, g)
                    else:
                        dve.wait_ge(s_sht, 1)
                    head_norm(num[g % 2][:, :, :], P, tok[:, 2, :, g], NJ, s_sq, g + 2, hs[:, :, :], s_hs)
                if h >= 2:
                    g = h - 2
                    dve.wait_ge(s_ht, g + 1)
                    V.tensor_tensor(prompt(og[:, g, :]), prompt(og[:, g, :]), B5[:, :].rearrange("p (h c) -> p h c", h=2),
                                    ALU.mult).then_inc(s_y, 1)
                    dve.wait_ge(s_y, g + 1)
                    V.tensor_copy(Xh[:, g, :], og[:, g, :]).then_inc(s_yh, 1)
            dve.wait_ge(s_back, 16 * KT)
            dve.wait_ge(s_out, 16 * STORES_STATE)
            dve.wait_ge(s_mod, 3)
            unit(G_WOUT, residual(2, 1))
            combine(5, 5, 5 * KT)
            norm_apply(1, 0, 1)
            dve.wait_ge(s_mod, 6)
            start = mids["n"]
            with dve.Fori(0, QUARTERS - 1) as j:
                unit(G_MLP0, drain_square(Hh, Hl, None), j, 16)
                combine(6, j + NMOD, j * KT + 6 * KT, j, 2)
                unit(G_MLP0 + 8, residual(5), j, 16)
                combine(7, j + (NMOD + 3), j * KT + 9 * KT, j, 2)
            assert mids["n"] - start == 16
            mids["n"] = start + 16 * (QUARTERS - 1)
            unit(G_MLP0_LAST, drain_square(Hh, Hl, None))
            unit(G_MLP0_LAST + 8, residual(5, 2))
            norm_apply(2, 1, 0)
            for m in range(KT):
                dve.wait_ge(s_ev, G_CG + m + 1)
                dve.wait_ge(s_dr, G_CG + m)
                V.memset(small_s[:, 0:1], 0.0).then_inc(s_dr, 1)
            dve.wait_ge(s_cre, 2)
            cw = lambda w, m: par1[:, 16 + w * KT + m:17 + w * KT + m]
            for m in range(KT):
                g = G_XT + m
                dve.wait_ge(s_ev, g + 1)
                dve.wait_ge(s_dr, g)
                s = stage[g % 2][:, :]
                up = u[:, m, 0:2 + SEQ]
                us = u[:, m, 2 + SEQ:UROW].rearrange("p (b t) -> p b t", t=2 + ST)
                V.tensor_tensor(up[:, 2:2 + SEQ].rearrange("p (h c) -> p h c", h=2),
                                up[:, 2:2 + SEQ].rearrange("p (h c) -> p h c", h=2), prompt(s), ALU.mult)
                us4 = us.rearrange("p (h b) t -> p h b t", h=2)
                chain.link(V.tensor_tensor(us4[:, :, :, 2:2 + ST], us4[:, :, :, 2:2 + ST], sample4(s), ALU.mult))
                yp = prompt(yc[:, m, :])
                ys = sample4(yc[:, m, :])
                ph = lambda w: up[:, w:w + SEQ].rearrange("p (h c) -> p h c", h=2)
                V.tensor_scalar(yp, ph(0), cw(0, m), None, ALU.mult)
                tmp = small_s[:, :].rearrange("p (b t) -> p b t", t=ST)
                chain.link(V.tensor_scalar(tmp, us[:, :, 0:ST], cw(0, m), None, ALU.mult))
                for w in (1, 2):
                    V.scalar_tensor_tensor(yp, ph(w), cw(w, m), yp, ALU.mult, ALU.add)
                    chain.link(V.scalar_tensor_tensor(tmp, us[:, :, w:w + ST], cw(w, m), tmp, ALU.mult, ALU.add))
                V.tensor_copy(sample(yc[:, m, :]), small_s[:, :].rearrange("p (h c) -> p h c", h=2))
                V.tensor_copy(ulast[:, m, 0:2], up[:, SEQ:SEQ + 2])
                V.tensor_copy(ulast[:, m, 2:2 * NSEQ].rearrange("p (b r) -> p b r", r=2), us[:, :, ST:ST + 2])\
                    .then_inc(s_dr, 1)
            dve.wait_ge(s_dr, G_BG)
            unit(G_BG, drain_square(Hh, Hl, yc))
            unit(G_COUT, residual(NMOD + 2, 3))
            norm_apply(3, 1, 1)
            start = mids["n"]
            with dve.Fori(0, QUARTERS - 1) as j:
                unit(G_MLP1, drain_square(Hh, Hl, None), j, 16)
                unit(G_MLP1 + 8, residual(NMOD + 5), j, 16)
            assert mids["n"] - start == 16
            mids["n"] = start + 16 * (QUARTERS - 1)
            unit(G_MLP1_LAST, drain_square(Hh, Hl, None))
            unit(G_MLP1_LAST + 8, residual(NMOD + 5, 4))
            dve.wait_ge(s_root, 5)
            chain.link(V.reciprocal(rstd[:, :], rstd[:, :]))
            for m in range(KT):
                if m >= 2:
                    dve.wait_ge(s_ft, m - 1)
                V.scalar_tensor_tensor(hb[m % 2][:, :], xT[:, m, :], par1[:, m:m + 1], rstd[:, :], ALU.mult, ALU.mult)\
                    .then_inc(s_fy, 1)

        @block.tensor
        def _(pe):
            mm = nc.tensor.matmul

            def turn(out, in_, n):
                return nc.tensor.transpose(out, in_, ident[0:n, 0:n])

            def tile(t, g, xh, xl, j, per_t, per_g, ready=None):
                s = t % SLOTS
                split_wait(pe, t, j, per_t)
                if g >= 2:
                    pe.wait_ge(s_ev, at(g - 1, j, per_g))
                for k in range(KT):
                    if ready is not None:
                        ready(k)
                    first, final = k == 0, k == KT - 1
                    for w, x, st, en in ((wh, xh, first, False), (wh, xl, False, False), (wl, xh, False, final)):
                        for hf in range(2):
                            last = mm(G[:, 2 * (g % 2) + hf, 0:HALF], w[:, s, k, :], x[:, k, hf * HALF:(hf + 1) * HALF],
                                      start=st, stop=en)
                last.then_inc(s_used, 1)

            def ada_pair(t, k, j=None, per_t=0, per_k=0):
                split_wait(pe, t, j, per_t)
                split_wait(pe, t + 1, j, per_t)
                if k >= 1:
                    pe.wait_ge(s_ae, at(k, j, per_k))
                s = t % SLOTS
                for kk in range(KT):
                    for w in (wh, wl):
                        last = mm(B4[0:2 * NSEQ, 0:2 * P], c2[:, kk, :], w[:, s:s + 2, kk, :],
                                  start=(kk == 0 and w is wh), stop=(kk == KT - 1 and w is wl))
                last.then_inc(s_used, 2)

            def ada_turn(n, j=None, per=0):
                if j is None:
                    pe.wait_ge(s_ae, 4 * (n + 1))
                for m in range(KT):
                    last = turn(B6[:, m * 2 * NSEQ:(m + 1) * 2 * NSEQ], modrow[:, m * P:(m + 1) * P], 2 * NSEQ)
                last.then_inc(s_tr, 1)

            def unit(t0, g0, xh, xl, j=None, per_t=0, per_g=0, ready=None):
                if j is None:
                    with pe.Fori(0, 2) as i:
                        for m in range(SLOTS):
                            tile(t0 + m, g0 + m, xh, xl, i, SLOTS, SLOTS, ready if m == 0 else None)
                    return
                for m in range(KT):
                    tile(t0 + m, g0 + m, xh, xl, j, per_t, per_g, ready if m == 0 else None)

            def mixed(t0, g0, n, xh, xl, ready, j=None, per_t=0, per_g=0, per_n=0, post=None):
                if j is None and post is None:
                    with pe.Fori(0, 2) as i:
                        for m in range(0, SLOTS, 2):
                            ada_pair(t0 + 2 * m, 4 * n + m // 2, i, 2 * SLOTS, 2)
                            for o in range(2):
                                tile(t0 + 2 * m + 2 + o, g0 + m + o, xh, xl, i, 2 * SLOTS, SLOTS,
                                     ready if m + o == 0 else None)
                    ada_turn(n)
                    return
                for m in range(0, KT, 2):
                    t = t0 + 2 * m
                    ada_pair(t, 4 * n + m // 2, j, per_t, 4 * per_n)
                    for i in range(2):
                        if j is not None and m + i == KT - 1:
                            pe.wait_ge(s_ae, at(4 * (n + 1), j, 4 * per_n))
                        tile(t + 2 + i, g0 + m + i, xh, xl, j, per_t, per_g, ready if m + i == 0 else None)
                        if post is not None:
                            post(m + i)
                ada_turn(n, j, per_n)

            def stats(n):
                pe.wait_ge(s_acc, n + 1)
                if n == 0:
                    pe.wait_ge(s_ptd, 1)
                mm(B5[:, 0:HALF], ones[:, :], acc[:, 0:HALF], start=True, stop=True)
                mm(B7[:, 0:HALF], ones[:, :], acc[:, HALF:TOK], start=True, stop=True).then_inc(s_stat, 1)

            def x_ready(x0):
                return lambda k: pe.wait_ge(s_kx, x0 + k + 1)

            def drained(g0, j=None, per=0):
                return lambda k: pe.wait_ge(s_dr, at(g0 + k + 1, j, per))

            pe.wait_ge(s_const, 1)
            pe.wait_ge(s_pin, 80)
            turn(B7[:, 0:P], parrow0[:, :], P)
            turn(B7[:, P:P + 40], parrow1[:, :], 40).then_inc(s_pt, 1)
            pe.wait_ge(s_silu, 2)
            for k in range(KT):
                last = turn(B5[:, k * NSEQ:(k + 1) * NSEQ], crow[:, 1, k * P:(k + 1) * P], NSEQ)
            last.then_inc(s_ct, 1)
            pe.wait_ge(s_xin, 80)
            for k in range(KT):
                last = turn(B6[:, k * NS:(k + 1) * NS], xin[0:NS, NJ, k * P:(k + 1) * P], NS)
            last.then_inc(s_xst, 1)
            for k in range(KT):
                if k >= 4:
                    pe.wait_ge(s_xe, k - 3)
                for jt in range(NJ):
                    last = turn(G[:, k % 4, jt * P:(jt + 1) * P], xin[:, jt, k * P:(k + 1) * P], P)
                last.then_inc(s_xt, 1)
            pe.wait_ge(s_cs, 1)
            for n, t0 in enumerate((T_ADA0, T_ADA1)):
                for m in range(0, KT, 2):
                    ada_pair(t0 + m, (t0 + m) // 2)
                if n == 0:
                    pe.wait_ge(s_xse, 1)
                ada_turn(n)
            stats(0)
            pe.wait_ge(s_gs, 2)
            pe.wait_ge(s_root, 1)
            pe.wait_ge(s_xe, KT)
            for k in range(KT):
                pe.wait_ge(s_kx, X_NORM0 + k + 1)
                for w, x, st, en in ((gh, Xh, k == 0, False), (gh, Xl, False, False), (gl, Xh, False, k == KT - 1)):
                    for hf, bank in enumerate((B5, B7)):
                        last = mm(bank[0:40, 0:HALF], w[:, k, :], x[:, k, hf * HALF:(hf + 1) * HALF], start=st, stop=en)
            last.then_inc(s_gp, 1)

            def post_k(m):
                if m == 3:
                    pe.wait_ge(s_ra, 3)
                    pe.wait_ge(s_rv, 3)
                    for i, r in enumerate((3, 1, 5)):
                        for jt in range(NJ):
                            c = (i * NJ + jt) * H
                            last = turn(B7[:, c:c + H], rows[r][:, col(jt * P):col(jt * P) + P], H)
                    last.then_inc(s_tt, 1)
                if m >= 5:
                    turn_k(m - 5)
                if m == 7:
                    turn_k(3)

            nt = {"n": 0}

            def turned_free():
                n = nt["n"]
                if n == 0:
                    pe.wait_ge(s_ttd, 1)
                elif n <= 4:
                    pe.wait_ge(s_vtd, n)
                else:
                    pe.wait_ge(s_dr, G_V + n - 4)
                nt["n"] += 1

            def turn_k(n):
                pe.wait_ge(s_dr, G_QK + 4 + n + 1)
                turned_free()
                for jt in range(NJ):
                    turn(B7[:, jt * P:(jt + 1) * P], kT[:, n, col(jt * P):col(jt * P) + P], P)
                turn(B5[0:NS, 0:P], ks[:, n, :], P).then_inc(s_vt, 1)

            def turn_v(m):
                pe.wait_ge(s_ev, G_V + m + 1)
                turned_free()
                st_ = stage[(G_V + m) % 2]
                for jt in range(NJ):
                    turn(B7[:, jt * P:(jt + 1) * P], st_[:, col(jt * P):col(jt * P) + P], P)
                turn(B5[0:NS, 0:P], vs[(G_V + m) % 2][:, :], P).then_inc(s_vt, 1)

            def post_v(m):
                if m >= 1:
                    turn_v(m - 1)
                if m == KT - 1:
                    turn_v(m)

            mixed(T_QK, G_QK, 2, Xh, Xl, None, post=post_k)
            mixed(T_V, G_V, 3, Xh, Xl, None, post=post_v)
            mixed(T_O, G_O, 4, Xh, Xl, None)
            pe.wait_ge(s_dr, G_O)
            pe.wait_ge(s_at, 5)
            for h in (*range(0, H, 2), *range(1, H, 2)):
                pr = slice(DK * (h % 2), DK * (h % 2) + DK)
                last = mm((B7, B6)[h % 2][0:NS, h // 2 * NS:(h // 2 + 1) * NS], ks[pr, h // 2, :], qs[pr, h // 2, :], start=True, stop=True)
            last.then_inc(s_ssc, 1)
            pe.wait_ge(s_sin, 16 * 2 * (SB + 1))
            pe.wait_ge(s_sp, 2)
            pe.wait_ge(s_ev, G_WOUT)
            for a in range(H // 2):
                for b in range(SB):
                    mm(G[0:2 * NS, a, 0:DVA], qbd[:, a, b, :], C0[:, b, a, :], start=(b == 0), stop=False)
                if a == 0:
                    pe.wait_ge(s_sp, 3)
                for h2 in range(2):
                    last = mm(G[0:2 * NS, a, 0:DVA], probs_s[:, 2 * a + h2, :], vtok_s[:, 2 * a + h2, :],
                              start=False, stop=(h2 == 1))
            last.then_inc(s_spv, 1)
            pe.wait_ge(s_ae, 20)
            for a in range(H // 2):
                for b in range(SB):
                    n = SB * a + b
                    pe.wait_ge(s_kam, 9 * a + 1 + (b - 1 if b >= 2 else 0))
                    mm((B4, B5)[n % 2][:, 0:2 * DVA], kam[:, b, :], vtok_s[:, 2 * a:2 * a + 2, :].rearrange("p h e -> p (h e)"),
                       start=True, stop=True).then_inc(s_cu, 1)
            pe.wait_ge(s_sp, 5)
            pe.wait_ge(s_at, 5)
            for a in range(H // 2):
                last = turn(B6[:, a * 2 * NS:(a + 1) * 2 * NS], hs[0:2 * NS, a, :], 2 * NS)
            last.then_inc(s_sht, 1)
            pe.wait_ge(s_cud, 1)
            pe.wait_ge(s_selr, 1)
            pe.wait_ge(s_snum, 1)
            for h in range(H + 2):
                if h < H:
                    hm, pr = h // 2, slice(DK * (h % 2), DK * (h % 2) + DK)
                    if h:
                        pe.wait_ge(s_d, NJ * h)
                    mm(B4[:, :], sel[:, h, :], negMp[:, :], start=True, stop=True).then_inc(s_bc, 1)
                    for i in range(NJ):
                        if h:
                            pe.wait_ge(s_pr, NJ * (h - 1) + i + 1)
                        t0 = P * i
                        for hf in range(2):
                            lo_, hi_ = max(t0, PH * hf), PH * (hf + 1)
                            if lo_ < hi_:
                                last = mm(G[:, i, lo_ - t0:hi_ - t0], kT[pr, hm, col(t0):col(t0) + P],
                                          qT[pr, hm, col(lo_):col(lo_) + hi_ - lo_], start=True, stop=True)
                        last.then_inc(s_s, 1)
                if 1 <= h <= H:
                    g = h - 1
                    pe.wait_ge(s_pr, NJ * (g + 1))
                    if g:
                        pe.wait_ge(s_num, g)
                    else:
                        pe.wait_ge(s_sp, 6)
                    for jt in range(NJ):
                        out = (B6, B7)[jt // 2][:, (jt % 2) * DVA:(jt % 2 + 1) * DVA]
                        o = 0
                        for i in range(jt + 1):
                            c = o + P * (jt - i)
                            last = mm(out, probs[g % 2][:, c:c + P], vtok[:, i, g, :], start=(i == 0), stop=(i == jt))
                            o += SEQ - P * i
                    last.then_inc(s_pv, 1)
                if h >= 2:
                    g = h - 2
                    pe.wait_ge(s_hs, g + 1)
                    if g:
                        pe.wait_ge(s_y, g)
                    for jt in range(NJ):
                        last = turn(B5[:, jt * P:(jt + 1) * P], hs[:, jt, :], P)
                    last.then_inc(s_ht, 1)
            for h in range(H):
                for i in range(NJ):
                    last = mm(G[0:DK, h // 3, (h % 3) * DVA:(h % 3 + 1) * DVA], ktok[:, i, h * DK:(h + 1) * DK],
                              vtok[:, i, h, :], start=(i == 0), stop=(i == NJ - 1))
            last.then_inc(s_cp, 1)
            pe.wait_ge(s_cpo, 1)
            mixed(T_WOUT, G_WOUT, 5, Xh, Xl, x_ready(X_Y))
            stats(1)
            MLP0_X = x_ready(X_NORM1)
            with pe.Fori(0, QUARTERS - 1) as j:
                mixed(T_MLP0, G_MLP0, 6, Xh, Xl, MLP0_X, j, 32, 16, 2)
                mixed(T_MLP0 + 16, G_MLP0 + 8, 7, Hh, Hl, drained(G_MLP0, j, 16), j, 32, 16, 2)
            unit(T_MLP0_LAST, G_MLP0_LAST, Xh, Xl, ready=MLP0_X)
            unit(T_MLP0_LAST + 8, G_MLP0_LAST + 8, Hh, Hl, ready=drained(G_MLP0_LAST))
            pe.wait_ge(s_crin, 16)
            pe.wait_ge(s_at, 12)
            for k in range(KT):
                last = turn(B6[:, k * 2 * SB:(k + 1) * 2 * SB], crows[:, k * P:(k + 1) * P], 2 * SB)
            last.then_inc(s_crt, 1)
            stats(2)
            unit(T_CG, G_CG, Xh, Xl, ready=x_ready(X_NORM2))
            unit(T_XT, G_XT, Xh, Xl, ready=x_ready(X_NORM2))
            unit(T_BG, G_BG, Xh, Xl, ready=x_ready(X_NORM2))
            pe.wait_ge(s_dr, G_BG)
            pe.wait_ge(s_cre, 2)
            for k in range(KT):
                last = mm((B4, B6)[k // 4][0:2 * NSEQ, (k % 4) * P:(k % 4 + 1) * P], ulast[:, k, :], ident[:, :],
                          start=True, stop=True, is_transpose=True)
            last.then_inc(s_ult, 1)
            unit(T_COUT, G_COUT, Hh, Hl, ready=drained(G_BG))
            stats(3)
            MLP1_X = x_ready(X_NORM3)
            with pe.Fori(0, QUARTERS - 1) as j:
                unit(T_MLP1, G_MLP1, Xh, Xl, j, 16, 16, ready=MLP1_X)
                unit(T_MLP1 + 8, G_MLP1 + 8, Hh, Hl, j, 16, 16, ready=drained(G_MLP1, j, 16))
            unit(T_MLP1_LAST, G_MLP1_LAST, Xh, Xl, ready=MLP1_X)
            unit(T_MLP1_LAST + 8, G_MLP1_LAST + 8, Hh, Hl, ready=drained(G_MLP1_LAST))
            stats(4)
            pe.wait_ge(s_ulo, 1)
            for m in range(KT):
                pe.wait_ge(s_fy, m + 1)
                if m >= 2:
                    pe.wait_ge(s_fo, m - 1)
                hm = hb[m % 2]
                for jt in range(NJ):
                    turn(G[:, m % 4, jt * P:(jt + 1) * P], hm[:, col(jt * P):col(jt * P) + P], P)
                for hf in range(2):
                    c = hf * HALF + PH
                    last = mm((B4, B6)[m % 2][0:SH, hf * P:(hf + 1) * P], hm[:, c:c + SH], ident[:, :],
                              start=True, stop=True, is_transpose=True)
                last.then_inc(s_ft, 1)


STORES_STATE = 2 * (SB + 1) + 2
N_STORES = STORES_STATE + 2 + KT + 1

_INS = ["x_prompt", "x_sample", "c_prompt", "c_sample", "state_mlstm_C", "state_mlstm_n", "state_mlstm_m", "state_conv",
        "ada_w", "ada_b", "norm_g", "final_norm_g", "mlstm_w_in", "mlstm_b_gates", "mlstm_head_g", "mlstm_w_out",
        "conv_w_in", "conv_w", "conv_w_out", "mlp_w_up", "mlp_w_down"]
_OUTS = [(1, SEQ, D), (SB, ST, D), (1, 1, H, DK, DV), (1, 1, H, DK), (1, 1, H), (1, 1, 2, D),
         (1, SB, H, DK, DV), (1, SB, H, DK), (1, SB, H), (1, SB, 2, D)]


def kernel(**inputs):
    import numpy as np
    import concourse.bacc as bacc
    from concourse.bass_utils import run_bass_kernel_spmd

    nc = bacc.Bacc("TRN2", target_bir_lowering=False, num_devices=1)
    arrays, args = {}, {}
    for name in _INS:
        a = np.ascontiguousarray(inputs[name])
        arrays[f"in_{name}"] = a
        args[name] = nc.dram_tensor(f"in_{name}", a.shape, mybir.dt.from_np(a.dtype), kind="ExternalInput").ap()
    outs = [nc.dram_tensor(f"out_{i}", s, F32, kind="ExternalOutput").ap() for i, s in enumerate(_OUTS)]
    build_program(nc, args, outs)
    r = run_bass_kernel_spmd(nc, [arrays], core_ids=[0])
    return tuple(r.results[0][f"out_{i}"] for i in range(len(_OUTS)))
```

```python
import concourse.bass as bass
from concourse import mybir
from contextlib import ExitStack

F32 = mybir.dt.float32
F32R = mybir.dt.float32r
ALU = mybir.AluOpType
ACT = mybir.ActivationFunctionType
AX = mybir.AxisListType

P = 128
D = 1024
KT = D // P
SEQ, SB, ST = 512, 8, 4
PH, SH = SEQ // 2, SB * ST // 2
HALF = PH + SH
TOK = 2 * HALF
NS = SB * ST
NSEQ = 1 + SB
H, DK, DV = 8, 64, 128
DVA = DV + 1
NJ = SEQ // P
EPS = 1e-6
STATE_TILE = 4
SSQ = 5
EARLY0, EARLY1 = 4, 12
SLOTS, LEAD = 4, 3
NMOD = 6
DFF = 4 * D
QUARTERS = DFF // D
CONVW = 3
UROW = 2 + SEQ + SB * (2 + ST)
LAST_COL = HALF + PH - 1

T_ADA0, T_ADA1 = 0, 8
T_QK, T_V, T_O, T_WOUT = 16, 32, 48, 64
T_MLP0, T_MLP0_LAST = 80, 176
T_CG, T_XT, T_BG, T_COUT = 192, 200, 208, 216
T_MLP1, T_MLP1_LAST, T_END = 224, 272, 288
G_QK, G_V, G_O, G_WOUT, G_MLP0, G_MLP0_LAST = 0, 8, 16, 24, 32, 80
G_CG, G_XT, G_BG, G_COUT, G_MLP1, G_MLP1_LAST = 96, 104, 112, 120, 128, 176
MIXED = ((0, 0), (1, 1), (2, None, 0), (4, 2), (5, 3), (6, None, 1), (8, 4), (9, 5), (10, None, 2),
         (12, 6), (13, None, 3), (15, 7))
VECTOR_LOWS = tuple(t + 15 for t in (T_O, T_WOUT, T_MLP0, T_MLP0 + 16))
X_AFTER = {0: (0, 1), 1: (2, 3), 2: (4, 5), 3: (6, 7)}
X_NORM0, X_Y, X_NORM1, X_NORM2, X_NORM3 = 0, 8, 16, 24, 32


class Count:

    def __init__(self, engine, sem):
        self.engine, self.sem, self.n = engine, sem, 0

    def link(self, ins):
        ins.then_inc(self.sem, 1)
        self.n += 1
        self.engine.wait_ge(self.sem, self.n)


def halves(ap):
    return ap.rearrange("p (h c) -> p h c", h=2)


def prompt(ap):
    return halves(ap)[:, :, 0:PH]


def sample(ap):
    return halves(ap)[:, :, PH:HALF]


def sample4(ap):
    return sample(ap).rearrange("p h (b t) -> p h b t", t=ST)


def col(t):
    return (t // PH) * HALF + t % PH


def build_program(nc, ins, outs):
    ctx = ExitStack()
    with ctx:
        base = (nc.sbuf_base + 63) // 64 * 64
        mark = {"at": base}

        def sb(name, shape, dt=F32, at=None):
            n = 4
            for s in shape[1:]:
                n *= s
            n = (n + 31) // 32 * 32
            if at is None:
                at = mark["at"]
                mark["at"] += n
            return nc.alloc_sbuf_tensor_at(name, shape, dt, offset=at)

        def region(nbytes):
            at = mark["at"]
            mark["at"] += (nbytes + 31) // 32 * 32
            return at

        def sem(name):
            return ctx.enter_context(nc.semaphore(name))

        ROW = TOK * 4
        at_x = region(KT * ROW)
        xT = sb("xT", [P, KT, TOK], at=at_x)
        NUMB = 2080
        PW = sum(SEQ - P * j for j in range(NJ))
        probs = [sb(f"probs{i}", [P, PW], at=at_x + i * PW * 4) for i in range(2)]
        num = [sb(f"num{i}", [P, NJ, DVA], at=at_x + 2 * PW * 4 + i * NUMB) for i in range(2)]
        at_s = at_x
        dec_s = sb("dec_s", [NS, H, NS], at=at_s)
        negM_s = sb("negM_s", [NS, H, NS], at=at_s + 1024)
        probs_s = sb("probs_s", [NS, H, 2 * NS], at=at_s + 2048)
        einter_s = sb("einter_s", [P, H // 2, NS], at=at_s + 4096)
        kam = [sb(f"kam{i}", [NS, SB, P], at=at_s + 4608 + i * SB * P * 4) for i in range(2)]
        num_s = sb("num_s", [2 * NS, H // 2, DVA], at=at_s + 4608 + 2 * SB * P * 4)
        ktok_s = sb("ktok_s", [NS, H * DK], at=at_s + 4608 + 2 * SB * P * 4 + NUMB)
        at_X = mark["at"]
        Xh = sb("Xh", [P, KT, TOK], F32R)
        Xl = sb("Xl", [P, KT, TOK], F32R)
        early = sb("early", [P, EARLY1 - EARLY0, KT, P], at=at_X)
        assert (EARLY1 - EARLY0) * D * 4 <= 2 * KT * ROW
        at_h = region(2 * KT * ROW)
        Hh = sb("Hh", [P, KT, TOK], F32R, at=at_h)
        Hl = sb("Hl", [P, KT, TOK], F32R, at=at_h + KT * ROW)
        xin = sb("xin", [P, NJ + 1, D], at=at_h)
        xn = sb("xn", [P, KT, TOK], at=at_h)
        vtok = sb("vtok", [P, NJ, H, DVA], at=at_h)
        C0 = sb("C0", [P, SB, H // 2, DVA], at=at_h + NJ * H * DVA * 4)
        at_t = at_h + (NJ + SB // 2) * H * DVA * 4
        qs = sb("qs", [P, H // 2, NS], at=at_t)
        ks = sb("ks", [P, H // 2, NS], at=at_t + 512)
        tok = sb("tok", [P, 3, NJ, H], at=at_t + 1024)
        yrow = sb("yrow", [P, NJ, D], at=at_h)
        yrow_s = sb("yrow_s", [SH, 2, D], at=at_h + NJ * D * 4)
        raw = sb("raw", [P, SLOTS, KT, P])
        wh = sb("wh", [P, SLOTS, KT, P], F32R)
        wl = sb("wl", [P, SLOTS, KT, P], F32R)
        modT = sb("modT", [P, 2 * NMOD, KT, NSEQ])
        gain = sb("gain", [P, KT, NSEQ])
        par0 = sb("par0", [P, P])
        par1 = sb("par1", [P, 40])
        ident = sb("ident", [P, P])
        ones = sb("ones", [P, P])
        c2 = sb("c2", [P, KT, 2 * NSEQ], F32R)
        at_row = region(D * 4)
        modrow = sb("modrow", [2 * NSEQ, D], at=at_row)
        sel = sb("sel", [H, H, P], at=at_row)
        modps = sb("modps", [P, KT, 2 * NSEQ])
        modsum = sb("modsum", [P, KT, NSEQ])
        stage = [sb(f"stage{i}", [P, TOK]) for i in range(2)]
        vs = [sb(f"vs{i}", [P, NS]) for i in range(2)]
        at_sq = region(ROW)
        sqb = sb("sqb", [P, TOK], at=at_sq)
        hs = sb("hs", [P, NJ, DV], at=at_sq)
        small_s = sb("small_s", [P, SH * 2])
        g_s = sb("g_s", [NS, H])
        a_s = sb("a_s", [NS, H])
        enm_s = sb("enm_s", [2 * NS, H // 2])
        stat = sb("stat", [P, 7, NJ])
        mhalf = sb("mhalf", [P, NJ + 1])
        rms = sb("rms", [P, 2, NJ + 1])
        mask_b = sb("mask_b", [NS, SB])
        bgate = sb("bgate", [P, 1])
        m0row = sb("m0row", [H, SB])
        at_n = region(5 * ROW)
        samp = sb("samp", [P, KT, NS], at=at_n)
        acc = sb("acc", [P, TOK], at=at_n + ROW)
        xr = sb("xr", [P, TOK], at=at_n + 2 * ROW)
        hb = [sb(f"hb{i}", [P, TOK], at=at_n + (3 + i) * ROW) for i in range(2)]
        diag = sb("diag", [P, NJ + 1, P], at=at_n + 3 * ROW)
        qbd = sb("qbd", [P, H // 2, SB, 2 * NS], at=at_n)
        negMp = sb("negMp", [H, SEQ], at=at_n + 8192)
        Cp = sb("Cp", [DK, H, DVA], at=at_n)
        at_f = region(2 * 4 * ROW + KT * ROW + NJ * H * DK * 4)
        qT = sb("qT", [P, H // 2, TOK], at=at_f)
        kT = sb("kT", [P, H // 2, TOK], at=at_f + 4 * ROW)
        og = sb("og", [P, KT, TOK], at=at_f + 8 * ROW)
        ktok = sb("ktok", [P, NJ, H * DK], at=at_f + 16 * ROW)
        vtok_s = sb("vtok_s", [NS, H, DVA])
        rows = [sb(f"rows{i}", [H, TOK], at=at_f + 8 * ROW + i * ROW) for i in range(6)]
        gw = 8 * 40 * 4
        graw = sb("graw", [P, KT, 40], at=at_f + 14 * ROW)
        gh = sb("gh", [P, KT, 40], F32R, at=at_f + 14 * ROW + gw)
        gl = sb("gl", [P, KT, 40], F32R, at=at_f + 14 * ROW + 2 * gw)
        crow = sb("crow", [NSEQ, D], at=at_f)
        parrow0 = sb("parrow0", [P, P], at=at_f + 12288)
        parrow1 = sb("parrow1", [40, P], at=at_f + 12288 + 512)
        ccol = sb("ccol", [P, KT, NSEQ], at=at_f + 12288 + 1024)
        cexp = sb("cexp", [P, KT, NSEQ], at=at_f + 12288 + 1024 + 512)
        u = sb("u", [P, KT, UROW], at=at_f)
        yc = sb("yc", [P, KT, TOK], at=at_f + KT * UROW * 4)
        crows = sb("crows", [2 * SB, D], at=at_f + KT * UROW * 4 + KT * ROW)
        urows = sb("urows", [2 * NSEQ, D], at=at_f + KT * UROW * 4 + KT * ROW)
        ulast = sb("ulast", [P, KT, 2 * NSEQ], at=at_f + KT * UROW * 4 + KT * ROW + D * 4)
        assert mark["at"] <= nc.sbuf_usable_end, mark["at"] - nc.sbuf_usable_end

        G = ctx.enter_context(nc.psum_tensor("G", [P, 4, 512], F32))
        B = ctx.enter_context(nc.psum_tensor("B", [P, 4, 512], F32))
        B4, B5, B7, B6 = [B[:, i, :] for i in range(4)]
        rstd = B[:, 1:3, 0:HALF]
        SUMS = 500

        def raw_of(t):
            return early[:, t - EARLY0] if EARLY0 <= t < EARLY1 else raw[:, t % SLOTS]

        def slot(g):
            return G[:, 2 * (g % 2):2 * (g % 2) + 2, 0:HALF]

        xspill = nc.dram_tensor("xspill", [P, KT * TOK], F32, kind="Internal").ap()
        bounce = nc.dram_tensor("bounce", [5, H, NS], F32, kind="Internal").ap()

        s_raw = [sem(f"raw_in{i}") for i in range(SLOTS)]
        s_early = [sem(f"early_in{i}") for i in range(EARLY1 - EARLY0)]
        s_hi = sem("hi_ready")
        s_lo = [sem("lo_even"), sem("lo_odd")]
        s_used = sem("tile_used")
        s_ev = sem("evacuated")
        s_dr = sem("drained")
        s_mid = sem("drain_mid")
        s_ae = sem("ada_pair_out")
        s_at = sem("ada_cols")
        s_tr = sem("ada_turned")
        s_cmb = sem("ada_mid")
        s_mod = sem("mod_ready")
        s_kx = sem("x_operand")
        s_hh = sem("norm_h")
        s_hhi = sem("norm_hi")
        s_vt = sem("kv_turned")
        s_vtd = sem("kv_turned_out")
        s_stat = sem("mean_square")
        s_sum = sem("squares_by_token")
        s_rms, s_diag = sem("rms_by_token"), sem("rms_diagonals")
        s_root = sem("rms_spread")
        s_sm, s_smh = sem("norm_sample"), sem("norm_sample_hi")
        s_acc = sem("squares_summed")
        s_v, s_a, s_p = sem("vector_chain"), sem("scalar_chain"), sem("gpsimd_chain")
        s_cin, s_xin, s_pin, s_gin, s_sin = sem("c_in"), sem("x_in"), sem("params_in"), sem("gates_in"), sem("state_in")
        s_const = sem("constants")
        s_silu = sem("silu_ready")
        s_ct, s_cs, s_pt, s_ptd = sem("c_turned"), sem("c_split"), sem("params_turned"), sem("params_out")
        s_xt, s_xe, s_xst, s_xse = sem("x_turned"), sem("x_stored"), sem("xs_turned"), sem("xs_stored")
        s_gs = sem("gates_split")
        s_gp, s_rv, s_ra = sem("gates_product"), sem("rows_vector"), sem("rows_scalar")
        s_spill, s_back = sem("x_spilled"), sem("x_back")
        s_bo, s_bi = sem("bounce_out"), sem("bounce_in")
        s_tt, s_ttd = sem("rows_turned"), sem("rows_turned_out")
        s_sd, s_sp = sem("sample_decay"), sem("sample_vector")
        s_ssc, s_spv, s_sht, s_snum = sem("sample_scores"), sem("sample_pv"), sem("sample_turned"), sem("sample_num")
        s_srs = sem("sample_rs")
        s_kam, s_cu, s_upd, s_cud = sem("kam_ready"), sem("state_product"), sem("state_updated"), sem("all_state_updated")
        s_old, s_oldout = sem("old_state_product"), sem("old_state_out")
        s_ssq = sem("head_squares_summed")
        s_selr = sem("selector")
        s_bc, s_s, s_d, s_sel, s_pr = sem("negM_spread"), sem("scores"), sem("decay"), sem("masked"), sem("probs_ready")
        s_pv, s_num, s_sq, s_rs, s_hs = sem("pv"), sem("num_out"), sem("squares"), sem("head_rs"), sem("hs_ready")
        s_ht, s_y, s_yh = sem("hs_turned"), sem("y_ready"), sem("y_hi")
        s_cp, s_cpo = sem("prompt_state"), sem("prompt_state_out")
        s_out = sem("stored")
        s_crin, s_crt, s_cre = sem("conv_rows_in"), sem("conv_rows_turned"), sem("conv_rows_out")
        s_ul, s_ult, s_ulo = sem("u_last"), sem("u_last_turned"), sem("u_last_out")
        s_fy, s_ft, s_fo = sem("final_y"), sem("final_turned"), sem("final_out")
        n_out = {"n": 0}

        ctx.enter_context(nc.allow_non_contiguous_dma(reason="a few small loads of single elements"))
        block = ctx.enter_context(nc.Block())

        def at(n, j, per):
            return n if j is None else j * per + n

        def split_wait(eng, t, j, per):
            eng.wait_ge(s_hi, at(t + 1, j, per))
            eng.wait_ge(s_lo[t % 2], at(t // 2 + 1, j, per // 2))

        @block.sync
        def _(sp):
            def fetch(t, w, c, j=None, per=0):
                if EARLY0 <= t < EARLY1:
                    nc.sync.dma_start(raw_of(t), w.rearrange("(k p) n -> p k n", p=P)[:, :, c:c + P])\
                        .then_inc(s_early[t - EARLY0], 16)
                    return
                if t >= EARLY1:
                    last = t - (SLOTS if t >= EARLY1 + SLOTS else EARLY1)
                    sp.wait_ge(s_lo[t % 2], at(last // 2 + 1, j, per // 2))
                nc.sync.dma_start(raw[:, t % SLOTS], w.rearrange("(k p) n -> p k n", p=P)[:, :, bass.ds(c, P)])\
                    .then_inc(s_raw[t % SLOTS], 16)

            def unit(t0, w, c0, j=None, per=0):
                for m in range(KT):
                    fetch(t0 + m, w, c0 + P * m, j, per)

            def mixed(t0, w, c0, wa, ca, j=None, per=0):
                mixed_part(MIXED, t0, w, c0, wa, ca, j, per)

            def mixed_part(order, t0, w, c0, wa, ca, j=None, per=0):
                for o, m, *pair in order:
                    if m is not None:
                        fetch(t0 + o, w, c0 + P * m, j, per)
                    else:
                        for i in range(2):
                            fetch(t0 + o + i, wa, ca + P * (2 * pair[0] + i), j, per)

            ada = [ins["ada_w"][layer] for layer in range(2)]
            w_in, w_out = ins["mlstm_w_in"][0], ins["mlstm_w_out"][0]
            nc.sync.dma_start(crow[0:1, :], ins["c_prompt"]).then_inc(s_cin, 16)
            nc.sync.dma_start(crow[1:NSEQ, :], ins["c_sample"]).then_inc(s_cin, 16)
            for m in range(2):
                fetch(T_ADA0 + m, ada[0], m * P)
            for j in range(NJ):
                nc.sync.dma_start(xin[:, j, :], ins["x_prompt"][0, j * P:(j + 1) * P, :]).then_inc(s_xin, 16)
            nc.sync.dma_start(xin[0:NS, NJ, :], ins["x_sample"].rearrange("b t n -> (b t) n")).then_inc(s_xin, 16)
            for m in range(2, KT):
                fetch(T_ADA0 + m, ada[0], m * P)
            unit(T_ADA1, ada[0], D)
            mixed(T_QK, w_in, 0, ada[0], 2 * D)
            sp.wait_ge(s_kx, X_NORM0 + KT)
            for h2 in range(2):
                for b in range(SB):
                    nc.sync.dma_start(C0[DK * h2:DK * (h2 + 1), b, :, 0:DV],
                                      ins["state_mlstm_C"][0, b].rearrange("(a h) d e -> h d a e", h=2)[h2]).then_inc(s_sin, 16)
                nc.sync.dma_start(C0[DK * h2:DK * (h2 + 1), :, :, DV:DVA].rearrange("p b a o -> p (b a) o"),
                                  ins["state_mlstm_n"][0].rearrange("b (a h) d -> h d (b a)", h=2)[h2]
                                  .rearrange("d (b o) -> d b o", o=1)).then_inc(s_sin, 16)
            mixed(T_V, w_in, D, ada[0], 3 * D)
            mixed(T_O, w_in, 2 * D, ada[0], 4 * D)
            mixed_part(MIXED[:3], T_WOUT, w_out, 0, ada[0], 5 * D)
            sp.wait_ge(s_cud, 1)
            for h2 in range(2):
                for b in range(SB):
                    nc.sync.dma_start(outs[6][0, b].rearrange("(a h) d e -> h d a e", h=2)[h2],
                                      C0[DK * h2:DK * (h2 + 1), b, :, 0:DV]).then_inc(s_out, 16)
                nc.sync.dma_start(outs[7][0].rearrange("b (a h) d -> h d (b a)", h=2)[h2].rearrange("d (b o) -> d b o", o=1),
                                  C0[DK * h2:DK * (h2 + 1), :, :, DV:DVA].rearrange("p b a o -> p (b a) o")).then_inc(s_out, 16)
            sp.wait_ge(s_y, H)
            sp.wait_ge(s_num, H)
            for k in range(KT):
                nc.sync.dma_start(xT[:, k, :], xspill[:, k * TOK:(k + 1) * TOK]).then_inc(s_back, 16)
            mixed_part(MIXED[3:], T_WOUT, w_out, 0, ada[0], 5 * D)
            up, down = ins["mlp_w_up"], ins["mlp_w_down"]

            def down_rows(layer, quarter):
                return down[layer, bass.ds(quarter * D, D), :]


            with sp.Fori(0, QUARTERS - 1) as j:
                mixed(T_MLP0, up[0], j * D + D, ada[1], j * D, j, 32)
                mixed(T_MLP0 + 16, down_rows(0, j + 1), 0, ada[1], j * D + 3 * D, j, 32)
            unit(T_MLP0_LAST, up[0], 0)
            unit(T_MLP0_LAST + 8, down_rows(0, 0), 0)
            cw = ins["conv_w_in"][0]
            unit(T_CG, cw, D)
            unit(T_XT, cw, 2 * D)
            unit(T_BG, cw, 0)
            unit(T_COUT, ins["conv_w_out"][0], 0)
            with sp.Fori(0, QUARTERS - 1) as j:
                unit(T_MLP1, up[1], j * D + D, j, 16)
                unit(T_MLP1 + 8, down_rows(1, j + 1), 0, j, 16)
            unit(T_MLP1_LAST, up[1], 0)
            unit(T_MLP1_LAST + 8, down_rows(1, 0), 0)
            for m in range(KT):
                sp.wait_ge(s_fo, m + 1)
                nc.sync.dma_start(outs[0][0].rearrange("(j p) n -> p j n", p=P)[:, :, m * P:m * P + P],
                                  yrow[:, :, m * P:m * P + P]).then_inc(s_out, 16)
            nc.sync.dma_start(outs[1].rearrange("(h b) t n -> (b t) h n", h=2), yrow_s[:, :, :]).then_inc(s_out, 16)
            sp.wait_ge(s_out, 16 * N_STORES)

        @block.scalar
        def _(act):
            chain = Count(act, s_a)

            def hi(t, j=None, per=0):
                if t >= T_END:
                    return
                if EARLY0 <= t < EARLY1:
                    act.wait_ge(s_early[t - EARLY0], 16)
                else:
                    passed = (EARLY1 - EARLY0) // SLOTS if t >= EARLY1 else 0
                    act.wait_ge(s_raw[t % SLOTS], at(16 * (t // SLOTS + 1 - passed), j, per // SLOTS * 16))
                if t >= SLOTS:
                    act.wait_ge(s_used, at(t - SLOTS + 1, j, per))
                nc.scalar.activation(wh[:, t % SLOTS], raw_of(t), ACT.Copy).then_inc(s_hi, 1)

            def to_stage(func, free=None, **kw):
                def evac(t, g, j, per_t, per_g):
                    act.wait_ge(s_used, at(t + 1, j, per_t))
                    if g >= 2:
                        act.wait_ge(s_dr, at(g - 1, j, per_g))
                    nc.scalar.activation(halves(stage[g % 2][:, :]), slot(g), func, **kw).then_inc(s_ev, 1)
                return evac

            def to_v(t, g, j, per_t, per_g):
                act.wait_ge(s_used, t + 1)
                act.wait_ge(s_dr, g - 1)
                nc.scalar.activation(vs[g % 2][:, :].rearrange("p (h c) -> p h c", h=2), slot(g)[:, :, PH:HALF], ACT.Copy)
                nc.scalar.activation(halves(stage[g % 2][:, :]), slot(g), ACT.Copy).then_inc(s_ev, 1)

            def to_qk(t, g, j, per_t, per_g):
                m = g - G_QK
                act.wait_ge(s_used, t + 1)
                dst = qT if m < 4 else kT
                nc.scalar.activation(halves(dst[:, m % 4, :]), slot(g), ACT.Copy).then_inc(s_ev, 1)

            def to_u(t, g, j, per_t, per_g):
                m = g - G_CG
                act.wait_ge(s_used, t + 1)
                ps = slot(g)
                nc.scalar.activation(u[:, m, 2:2 + SEQ].rearrange("p (h c) -> p h c", h=2),
                                     ps[:, :, 0:PH], ACT.Copy)
                nc.scalar.activation(
                    u[:, m, 2 + SEQ:UROW].rearrange("p (h b t) -> p h b t", h=2, t=2 + ST)[:, :, :, 2:2 + ST],
                    ps[:, :, PH:HALF].rearrange("p h (b t) -> p h b t", t=ST), ACT.Copy).then_inc(s_ev, 1)

            def ada_pair(t, pair, k, j=None, per_t=0, per_k=0):
                act.wait_ge(s_used, at(t + 2, j, per_t))
                if k >= 4:
                    act.wait_ge(s_tr, at(k // 4, j, per_k // 4))
                nc.scalar.activation(modrow[:, 2 * P * pair:2 * P * (pair + 1)], B4[0:2 * NSEQ, 0:2 * P], ACT.Copy)\
                    .then_inc(s_ae, 1)

            def ada_cols(n, j=None, per=0):
                act.wait_ge(s_tr, at(n + 1, j, per))
                if n >= 1:
                    act.wait_ge(s_cmb, at(n, j, per))
                nc.scalar.activation(modps[:, :, :], B6[:, 0:KT * 2 * NSEQ].rearrange("p (k c) -> p k c", k=KT),
                                     ACT.Copy).then_inc(s_at, 1)

            def unit(t0, g0, evac, j=None, per_t=0, per_g=0):
                for m in range(KT):
                    hi(t0 + m + LEAD, j, per_t)
                    evac(t0 + m, g0 + m, j, per_t, per_g)

            def mixed(t0, g0, n, evac, j=None, per_t=0, per_g=0, per_n=0, after={}):
                for o, m, *pair in MIXED:
                    t = t0 + o
                    if t != T_QK and m != 1:
                        hi(t + LEAD, j, per_t)
                    if m == 0:
                        hi(t + 1 + LEAD, j, per_t)
                    if m is None:
                        hi(t + 1 + LEAD, j, per_t)
                        ada_pair(t, pair[0], 4 * n + pair[0], j, per_t, 4 * per_n)
                        continue
                    evac(t, g0 + m, j, per_t, per_g)
                    if m in after:
                        after[m]()
                ada_cols(n, j, per_n)

            def norm_hi(n, layer, which):
                def samples():
                    act.wait_ge(s_sm, n + 1)
                    nc.scalar.activation(Xh[:, :, :].rearrange("p k (h c) -> p k h c", h=2)[:, :, :, PH:HALF],
                                         samp[:, :, :].rearrange("p k (h c) -> p k h c", h=2), ACT.Copy).then_inc(s_smh, 1)
                sc, sh = layer * NMOD + 3 * which + 1, layer * NMOD + 3 * which
                if n == 0:
                    samples()
                for k in range(KT):
                    if n == 0:
                        nc.scalar.activation(prompt(Xh[:, k, :]), prompt(xn[:, k, :]), ACT.Identity,
                                             bias=modT[:, sh, k, 0:1], scale=gain[:, k, 0:1]).then_inc(s_hhi, 1)
                        continue
                    act.wait_ge(s_hh, KT * (n - 1) + k + 1)
                    nc.scalar.activation(prompt(Xh[:, k, :]), prompt(hb[k % 2][:, :]), ACT.Identity,
                                         bias=modT[:, sh, k, 0:1]).then_inc(s_hhi, 1)
                    if k == 0:
                        samples()

            pin = [(parrow0[0:96, :], ins["ada_b"].rearrange("l (a p) -> (l a) p", p=P)),
                   (parrow0[96:128, :], ins["norm_g"].rearrange("l w (a p) -> (l w a) p", p=P)),
                   (parrow1[0:8, :], ins["final_norm_g"].rearrange("(a p) -> a p", p=P)),
                   (parrow1[8:16, :], ins["mlstm_head_g"].rearrange("l (a p) -> (l a) p", p=P)),
                   (parrow1[16:40, :], ins["conv_w"].rearrange("l w (a p) -> (l w a) p", p=P))]
            for dst, src in pin:
                nc.scalar.dma_start(dst, src).then_inc(s_pin, 16)
            act.wait_ge(s_ct, 1)
            nc.scalar.activation(cexp[:, :, :], B5[:, 0:KT * NSEQ].rearrange("p (k c) -> p k c", k=KT), ACT.Exp,
                                 scale=-1.0).then_inc(s_silu, 1)
            for t in range(LEAD):
                hi(t)
            for n, t0 in enumerate((T_ADA0, T_ADA1)):
                for m in range(0, KT, 2):
                    t = t0 + m
                    hi(t + LEAD)
                    hi(t + 1 + LEAD)
                    ada_pair(t, m // 2, t // 2)
                    for k in X_AFTER.get(t // 2, ()):
                        act.wait_ge(s_xt, k + 1)
                        nc.scalar.activation(prompt(xT[:, k, :]), G[:, k % 4, :].rearrange("p (h c) -> p h c", h=2),
                                             ACT.Copy).then_inc(s_xe, 1)
                    if t == T_ADA1 + 4:
                        act.wait_ge(s_gin, 80)
                        nc.scalar.activation(gh[:, :, :], graw[:, :, :], ACT.Copy).then_inc(s_gs, 1)
                ada_cols(n)
            norm_hi(0, 0, 0)
            hi(T_QK + LEAD)
            nc.scalar.dma_start(xspill, xT[:, :, :].rearrange("p k c -> p (k c)")).then_inc(s_spill, 16)
            act.wait_ge(s_rv, 1)
            chain.link(nc.scalar.activation(rows[1][:, :], rows[0][:, :], ACT.Exp, scale=-1.0))
            nc.scalar.activation(rows[2][:, :], rows[1][:, :], ACT.Ln, bias=1.0).then_inc(s_ra, 1)

            def rows_prompt():
                act.wait_ge(s_rv, 2)
                nc.scalar.activation(rows[5][:, :], rows[0][:, :], ACT.Exp, scale=-1.0).then_inc(s_ra, 1)
                for hf in range(2):
                    nc.scalar.activation(rows[1][:, hf * HALF:hf * HALF + PH], rows[3][:, hf * HALF:hf * HALF + PH],
                                         ACT.Exp, bias=rows[4][:, LAST_COL:LAST_COL + 1])

            def rows_sample():
                act.wait_ge(s_rv, 3)
                nc.scalar.activation(sample(rows[1][:, :]), sample(rows[1][:, :]), ACT.Exp)
                nc.scalar.activation(sample(rows[2][:, :]), sample(rows[2][:, :]), ACT.Exp).then_inc(s_ra, 1)

            def bounce_out():
                act.wait_ge(s_ra, 3)
                for i, r in enumerate((3, 1, 5, 4, 2)):
                    nc.scalar.dma_start(bounce[i].rearrange("h (a c) -> h a c", a=2), sample(rows[r][:, :])).then_inc(s_bo, 16)
                nc.scalar.dma_start(outs[4][0, 0, :].rearrange("(h o) -> h o", o=1), rows[0][:, LAST_COL:LAST_COL + 1])\
                    .then_inc(s_bo, 16)
                for hf in range(2):
                    nc.scalar.dma_start(outs[8][0, 4 * hf:4 * hf + 4].rearrange("b h -> h b"),
                                        sample4(rows[0][:, :])[:, hf, :, ST - 1]).then_inc(s_bo, 16)

            def bounce_in():
                act.wait_ge(s_bo, 16 * 8)
                by_token = lambda i: bounce[i].rearrange("h s -> s h")
                nc.scalar.dma_start(g_s[:, :], by_token(0)).then_inc(s_bi, 16)
                nc.scalar.dma_start(a_s[:, :], by_token(1)).then_inc(s_bi, 16)
                act.wait_ge(s_spill, 16)
                act.wait_ge(s_kx, X_NORM0 + 8)
                nc.scalar.dma_start(negM_s[:, :, :], bounce[3:4].rearrange("o h s -> o (h s)").broadcast_to((NS, H * NS))
                                    .rearrange("p (h s) -> p h s", h=H)).then_inc(s_bi, 16)
                for h2 in range(2):
                    pair = bounce[2].rearrange("(a h) s -> h s a", h=2)
                    nc.scalar.dma_start(enm_s[NS * h2:NS * (h2 + 1), :], pair[h2]).then_inc(s_bi, 16)
                    pair = bounce[4:5].rearrange("o (a h) s -> h o a s", h=2)
                    nc.scalar.dma_start(einter_s[DK * h2:DK * (h2 + 1), :, :],
                                        pair[h2].broadcast_to((DK, H // 2, NS))).then_inc(s_bi, 16)

            def sample_decay():
                act.wait_ge(s_sp, 1)
                nc.scalar.activation(dec_s[:, :, :], dec_s[:, :, :], ACT.Exp).then_inc(s_sd, 1)

            mixed(T_QK, G_QK, 2, to_qk, after={0: rows_prompt, 1: rows_sample, 2: bounce_out, 4: bounce_in})
            mixed(T_V, G_V, 3, to_v)
            def old_state_out():
                act.wait_ge(s_old, 1)
                nc.scalar.activation(num_s[:, 0:3, :], B5[0:2 * NS, 0:3 * DVA].rearrange("p (a e) -> p a e", a=3), ACT.Copy)
                nc.scalar.activation(num_s[:, 3, :], B7[0:2 * NS, 0:DVA], ACT.Copy).then_inc(s_oldout, 1)

            mixed(T_O, G_O, 4, to_stage(ACT.Exp, scale=-1.0), after={0: sample_decay, 3: old_state_out})
            act.wait_ge(s_snum, 1)
            for h in range(H + 1):
                if h < H:
                    act.wait_ge(s_bc, h + 1)
                    if h >= 2:
                        act.wait_ge(s_pv, h - 1)
                    o = 0
                    for i in range(NJ):
                        w = SEQ - P * i
                        nc.scalar.activation(probs[h % 2][:, o:o + w], B4[:, P * i:SEQ], ACT.Exp,
                                             bias=tok[:, 0, i, h:h + 1]).then_inc(s_d, 1)
                        o += w
                if h >= 1:
                    act.wait_ge(s_pv, h)
                    if h >= 3:
                        act.wait_ge(s_hs, h - 2)
                    else:
                        act.wait_ge(s_sp, 5)
                    for half in range(2):
                        last = nc.scalar.activation(num[(h - 1) % 2][:, 2 * half:2 * half + 2, :],
                                                    (B6, B7)[half][:, 0:2 * DVA].rearrange("p (j e) -> p j e", j=2), ACT.Copy)
                    last.then_inc(s_num, 1)
                    act.wait_ge(s_num, h)
                    if h >= 2:
                        act.wait_ge(s_ssq, h - 1)
                    for j in range(NJ):
                        last = nc.scalar.activation(stage[0][:, j * DV:(j + 1) * DV], num[(h - 1) % 2][:, j, 0:DV], ACT.Square,
                                                    accum_out=stat[:, SSQ + (h - 1) % 2, j:j + 1])
                    last.then_inc(s_ssq, 1)
            act.wait_ge(s_cp, 1)
            for b in range(3):
                n = min(3, H - 3 * b)
                last = nc.scalar.activation(Cp[:, 3 * b:3 * b + n, :],
                                            G[0:DK, b, 0:n * DVA].rearrange("p (h e) -> p h e", h=n), ACT.Copy)
            last.then_inc(s_cpo, 1)
            act.wait_ge(s_cpo, 1)
            nc.scalar.dma_start(outs[2][0, 0].rearrange("h d e -> d h e"), Cp[:, :, 0:DV]).then_inc(s_out, 16)
            nc.scalar.dma_start(outs[3][0, 0].rearrange("h (d o) -> d h o", o=1), Cp[:, :, DV:DVA]).then_inc(s_out, 16)
            mixed(T_WOUT, G_WOUT, 5, to_stage(ACT.Copy))
            norm_hi(1, 0, 1)
            with act.Fori(0, QUARTERS - 1) as j:
                mixed(T_MLP0, G_MLP0, 6, to_stage(ACT.Relu), j, 32, 16, 2)
                mixed(T_MLP0 + 16, G_MLP0 + 8, 7, to_stage(ACT.Copy), j, 32, 16, 2)
            unit(T_MLP0_LAST, G_MLP0_LAST, to_stage(ACT.Relu))
            nc.scalar.dma_start(crows[:, :], ins["state_conv"][0].rearrange("b r n -> (b r) n")).then_inc(s_crin, 16)
            unit(T_MLP0_LAST + 8, G_MLP0_LAST + 8, to_stage(ACT.Copy))
            norm_hi(2, 1, 0)
            act.wait_ge(s_crt, 1)
            nc.scalar.activation(
                u[:, :, 2 + SEQ:UROW].rearrange("p k (b t) -> p k b t", t=2 + ST)[:, :, :, 0:2],
                B6[:, 0:KT * 2 * SB].rearrange("p (k b r) -> p k b r", k=KT, r=2), ACT.Copy).then_inc(s_cre, 1)
            unit(T_CG, G_CG, to_u)
            unit(T_XT, G_XT, to_stage(ACT.Copy))
            unit(T_BG, G_BG, to_stage(ACT.Copy))
            act.wait_ge(s_ult, 1)
            for i, bank in enumerate((B4, B6)):
                last = nc.scalar.activation(urows[:, i * 512:(i + 1) * 512], bank[0:2 * NSEQ, :], ACT.Copy)
            last.then_inc(s_ulo, 1)
            act.wait_ge(s_ulo, 1)
            nc.scalar.dma_start(outs[5][0, 0], urows[0:2, :]).then_inc(s_out, 16)
            nc.scalar.dma_start(outs[9][0].rearrange("b r n -> (b r) n"), urows[2:2 * NSEQ, :]).then_inc(s_out, 16)
            unit(T_COUT, G_COUT, to_stage(ACT.Copy))
            norm_hi(3, 1, 1)
            with act.Fori(0, QUARTERS - 1) as j:
                unit(T_MLP1, G_MLP1, to_stage(ACT.Relu), j, 16, 16)
                unit(T_MLP1 + 8, G_MLP1 + 8, to_stage(ACT.Copy), j, 16, 16)
            unit(T_MLP1_LAST, G_MLP1_LAST, to_stage(ACT.Relu))
            unit(T_MLP1_LAST + 8, G_MLP1_LAST + 8, to_stage(ACT.Copy))
            for m in range(KT):
                act.wait_ge(s_ft, m + 1)
                nc.scalar.activation(yrow[:, :, m * P:m * P + P], G[:, m % 4, :].rearrange("p (j c) -> p j c", j=NJ), ACT.Copy)
                nc.scalar.activation(yrow_s[:, :, m * P:m * P + P],
                                     (B4, B6)[m % 2][0:SH, 0:2 * P].rearrange("p (j c) -> p j c", j=2), ACT.Copy).then_inc(s_fo, 1)

        @block.gpsimd
        def _(pool):
            chain = Count(pool, s_p)

            def lo(t, j=None, per=0):
                if t >= T_END:
                    return
                pool.wait_ge(s_hi, at(t + 1, j, per))
                nc.gpsimd.tensor_tensor(wl[:, t % SLOTS], raw_of(t), wh[:, t % SLOTS].bitcast(F32),
                                        ALU.subtract).then_inc(s_lo[t % 2], 1)

            def lows(t0, t1, j=None, per=0):
                for t in range(t0, t1):
                    if t in VECTOR_LOWS:
                        continue
                    if t - 2 in VECTOR_LOWS:
                        pool.wait_ge(s_lo[t % 2], at(t // 2, j, per // 2))
                    lo(t, j, per)

            def norm_power(n):
                pool.wait_ge(s_stat, n + 1)
                nc.gpsimd.tensor_tensor(rms[:, 1, :], rms[:, 0, :], mhalf[:, :], ALU.pow).then_inc(s_rms, 1)

            chain.link(nc.gpsimd.memset(ident[:, :], 0.0))
            nc.gpsimd.affine_select(out=ident[:, :], in_=ident[:, :], compare_op=ALU.not_equal, fill=1.0, base=0,
                                    pattern=[[-1, P]], channel_multiplier=1)
            nc.gpsimd.memset(mhalf[:, :], -0.5)
            nc.gpsimd.memset(ones[:, :], 1.0)
            chain.link(nc.gpsimd.memset(mask_b[:, :], 1.0))
            chain.link(nc.gpsimd.affine_select(out=mask_b[:, :], in_=mask_b[:, :], compare_op=ALU.is_ge, fill=0.0, base=0,
                                               pattern=[[-ST, SB]], channel_multiplier=1))
            chain.link(nc.gpsimd.affine_select(out=mask_b[:, :], in_=mask_b[:, :], compare_op=ALU.is_ge, fill=0.0, base=ST - 1,
                                               pattern=[[ST, SB]], channel_multiplier=-1))
            nc.gpsimd.memset(graw[:, :, :], 0.0).then_inc(s_const, 1)
            pool.wait_ge(s_const, 1)
            gates = ins["mlstm_w_in"][0].rearrange("(k p) n -> p k n", p=P)[:, :, 3 * D:3 * D + 2 * H]
            nc.gpsimd.dma_start(graw[:, :, 0:H], gates[:, :, 0:H]).then_inc(s_gin, 16)
            nc.gpsimd.dma_start(graw[:, :, 32:32 + H], gates[:, :, H:2 * H]).then_inc(s_gin, 16)
            bg = ins["mlstm_b_gates"].rearrange("o (g h) -> g h o", g=2)
            nc.gpsimd.dma_start(bgate[0:H, :], bg[0]).then_inc(s_gin, 16)
            nc.gpsimd.dma_start(bgate[32:32 + H, :], bg[1]).then_inc(s_gin, 16)
            nc.gpsimd.dma_start(m0row[:, :], ins["state_mlstm_m"][0].rearrange("b h -> h b")).then_inc(s_gin, 16)
            for t in range(T_ADA0 + 1, T_QK, 2):
                lo(t)
                if t == T_ADA1 + 3:
                    norm_power(0)
            for t in range(T_QK, T_QK + LEAD):
                pool.wait_ge(s_lo[0], T_QK // 2)
                lo(t)
            lows(T_QK + LEAD, T_V)
            pool.wait_ge(s_bi, 16 * 7)
            nc.gpsimd.memset(probs_s[:, :, :], 0.0)
            nc.gpsimd.memset(qbd[:, :, :, :], 0.0).then_inc(s_srs, 1)
            nc.gpsimd.memset(vtok_s[:, :, DV:DVA], 1.0)
            lows(T_V, T_O + 5)
            pool.wait_ge(s_sd, 1)
            dv = dec_s[:, :, :].rearrange("p h (b t) -> p h b t", t=ST)
            masks = 0
            for pattern, b0, cm in (([[0, H], [-ST, SB], [0, ST]], 0, 1),
                                    ([[0, H], [ST, SB], [0, ST]], ST - 1, -1),
                                    ([[0, H], [ST, SB], [1, ST]], 0, -1)):
                nc.gpsimd.affine_select(out=dv, in_=dv, compare_op=ALU.is_ge, fill=0.0, base=b0, pattern=pattern,
                                        channel_multiplier=cm).then_inc(s_srs, 1)
                masks += 1
                pool.wait_ge(s_srs, 1 + masks)
            def masked_keys(a):
                if a >= 2:
                    pool.wait_ge(s_cu, SB * (a - 1))
                nc.gpsimd.tensor_tensor(kam[a % 2][:, :, :], ktok_s[:, a * P:(a + 1) * P].unsqueeze(1).broadcast_to((NS, SB, P)),
                                        mask_b[:, :].unsqueeze(2).broadcast_to((NS, SB, P)), ALU.mult).then_inc(s_kam, 1)

            lows(T_O + 5, T_O + 8)
            masked_keys(0)
            lows(T_O + 8, T_O + 10)
            masked_keys(1)
            lows(T_O + 10, T_O + 13)
            masked_keys(2)
            lows(T_O + 13, T_O + 14)
            masked_keys(3)
            lows(T_O + 14, T_WOUT)
            pool.wait_ge(s_tr, 5)
            chain.link(nc.gpsimd.memset(sel[:, :, :], 0.0))
            nc.gpsimd.affine_select(out=sel[:, :, :], in_=sel[:, :, :], compare_op=ALU.not_equal, fill=1.0, base=0,
                                    pattern=[[-1, H], [0, P]], channel_multiplier=1).then_inc(s_selr, 1)
            lows(T_WOUT, T_WOUT + LEAD)
            pool.wait_ge(s_sp, 4)
            nc.gpsimd.tensor_tensor(stat[0:2 * NS, 3, :], stat[0:2 * NS, 2, :], mhalf[0:2 * NS, 0:NJ], ALU.pow).then_inc(s_rs, 1)
            for h in range(H + 2):
                if h < H:
                    o = 0
                    for i in range(NJ):
                        pool.wait_ge(s_d, NJ * h + i + 1)
                        diag = probs[h % 2][:, o:o + P]
                        nc.gpsimd.affine_select(out=diag, in_=diag, compare_op=ALU.is_ge, fill=0.0, base=0,
                                                pattern=[[1, P]], channel_multiplier=-1).then_inc(s_sel, 1)
                        o += SEQ - P * i
                if 1 <= h <= H:
                    pool.wait_ge(s_sq, h)
                    nc.gpsimd.tensor_tensor(stat[:, 3, :], stat[:, 2, :], mhalf[:, 0:NJ], ALU.pow).then_inc(s_rs, 1)
                if h >= 2:
                    g = h - 2
                    pool.wait_ge(s_yh, g + 1)
                    nc.gpsimd.tensor_tensor(Xl[:, g, :], og[:, g, :], Xh[:, g, :].bitcast(F32), ALU.subtract)\
                        .then_inc(s_kx, 1)
            lows(T_WOUT + LEAD, T_MLP0 + LEAD)
            norm_power(1)
            with pool.Fori(0, QUARTERS - 1) as j:
                lows(T_MLP0 + LEAD, T_MLP0 + LEAD + 32, j, 32)
            lows(T_MLP0_LAST + LEAD, T_CG + LEAD)
            norm_power(2)
            nc.gpsimd.memset(u[:, :, 0:2], 0.0).then_inc(s_cre, 1)
            lows(T_CG + LEAD, T_MLP1 + LEAD)
            norm_power(3)
            with pool.Fori(0, QUARTERS - 1) as j:
                lows(T_MLP1 + LEAD, T_MLP1 + LEAD + 16, j, 16)
            lows(T_MLP1_LAST + LEAD, T_END)
            norm_power(4)

        @block.vector
        def _(dve):
            chain = Count(dve, s_v)
            V = nc.vector
            mids = {"n": 0}

            def mid(ins_, j=None, per=0):
                ins_.then_inc(s_mid, 1)
                mids["n"] += 1
                dve.wait_ge(s_mid, at(mids["n"], j, per))

            def drain_square(hi_out, lo_out, other):
                def drain(m, g, j, per):
                    dve.wait_ge(s_ev, at(g + 1, j, per))
                    dve.wait_ge(s_dr, at(g, j, per))
                    s = stage[g % 2][:, :]
                    o = s if other is None else other[:, m, :]
                    V.tensor_tensor(hi_out[:, m, :], s, o, ALU.mult)
                    mid(V.tensor_tensor(sqb[:, :], s, o, ALU.mult), j, per)
                    V.tensor_tensor(lo_out[:, m, :], sqb[:, :], hi_out[:, m, :].bitcast(F32), ALU.subtract)\
                        .then_inc(s_dr, 1)
                return drain

            def residual(gate, stats_before=None):
                def drain(m, g, j, per):
                    dve.wait_ge(s_ev, at(g + 1, j, per))
                    dve.wait_ge(s_dr, at(g, j, per))
                    s = stage[g % 2][:, :]
                    gt = modT[:, gate, m, :]
                    V.scalar_tensor_tensor(prompt(xT[:, m, :]), prompt(s), gt[:, 0:1], prompt(xT[:, m, :]),
                                           ALU.mult, ALU.add)
                    mid(V.tensor_tensor(
                        small_s[:, :].rearrange("p (h b t) -> p h b t", h=2, t=ST), sample4(s),
                        gt[:, 1:NSEQ].rearrange("p (h b) -> p h b", h=2).unsqueeze(3).broadcast_to((P, 2, ST, ST)),
                        ALU.mult), j, per)
                    V.tensor_tensor(sample(xT[:, m, :]), sample(xT[:, m, :]),
                                    small_s[:, :].rearrange("p (h c) -> p h c", h=2), ALU.add).then_inc(s_dr, 1)
                    if stats_before is not None:
                        dve.wait_ge(s_dr, g + 1)
                        squares(m, stats_before)
                return drain

            def squares(m, n):
                if m == 0:
                    if n >= 1:
                        dve.wait_ge(s_kx, (X_NORM0, X_NORM1, X_NORM2, X_NORM3)[n - 1] + KT)
                    chain.link(V.tensor_tensor(acc[:, :], xT[:, m, :], xT[:, m, :], ALU.mult))
                else:
                    chain.link(V.tensor_tensor(sqb[:, :], xT[:, m, :], xT[:, m, :], ALU.mult))
                    ins_ = V.tensor_tensor(acc[:, :], acc[:, :], sqb[:, :], ALU.add)
                    if m == KT - 1:
                        ins_.then_inc(s_acc, 1)
                    else:
                        chain.link(ins_)

            def unit(g0, drain, j=None, per=0, low=None, per_t=0):
                for m in range(KT):
                    drain(m, g0 + m, j, per)
                    if low is not None and m == 5:
                        dve.wait_ge(s_hi, at(low + 1, j, per_t))
                        dve.wait_ge(s_lo[low % 2], at(low // 2, j, per_t // 2))
                        V.tensor_tensor(wl[:, low % SLOTS], raw[:, low % SLOTS], wh[:, low % SLOTS].bitcast(F32),
                                        ALU.subtract).then_inc(s_lo[low % 2], 1)

            def combine(n, dst, bias_col, j=None, per=0):
                dve.wait_ge(s_at, at(n + 1, j, per))
                if n >= 1:
                    dve.wait_ge(s_mod, at(n, j, per))
                V.tensor_tensor(modsum[:, :, :], modps[:, :, 0:NSEQ], modps[:, :, NSEQ:2 * NSEQ], ALU.add)\
                    .then_inc(s_cmb, 1)
                dve.wait_ge(s_cmb, at(n + 1, j, per))
                V.tensor_tensor(modT[:, dst, :, :], modsum[:, :, :],
                                par0[:, bass.ds(bias_col, KT)].unsqueeze(2).broadcast_to((P, KT, NSEQ)), ALU.add)\
                    .then_inc(s_mod, 1)

            def norm_diag(n):
                dve.wait_ge(s_sum, n + 1)
                V.tensor_scalar(rms[:, 0, :], B6[:, SUMS:SUMS + NJ + 1], 1.0 / D, EPS, ALU.mult, ALU.add).then_inc(s_stat, 1)
                dve.wait_ge(s_rms, n + 1)
                V.tensor_tensor(diag[:, :, :], ident[:, :].unsqueeze(1).broadcast_to((P, NJ + 1, P)),
                                rms[:, 1, :].unsqueeze(2).broadcast_to((P, NJ + 1, P)), ALU.mult).then_inc(s_diag, 1)

            seq_cols = lambda t: t[:, :, 1:NSEQ].unsqueeze(3).broadcast_to((P, KT, SB, ST))
            samples_of = lambda t: t[:, :, :].rearrange("p k (h c) -> p k h c", h=2)[:, :, :, PH:HALF]
            X_OF = (X_NORM0, X_NORM1, X_NORM2, X_NORM3)

            def norm_gain(n, layer, which):
                sc = layer * NMOD + 3 * which + 1
                dve.wait_ge(s_mod, (2, 5, 12, 12)[n])
                if n >= 1:
                    dve.wait_ge(s_kx, X_OF[n - 1] + KT)
                chain.link(V.tensor_scalar(gain[:, :, :], modT[:, sc, :, :], 1.0, None, ALU.add))
                gcol = 96 + (layer * 2 + which) * KT
                chain.link(V.tensor_tensor(gain[:, :, :], gain[:, :, :],
                                           par0[:, gcol:gcol + KT].unsqueeze(2).broadcast_to((P, KT, NSEQ)), ALU.mult))

            def norm_samples(n, layer, which):
                sh = layer * NMOD + 3 * which
                by_seq = samp[:, :, :].rearrange("p k (b t) -> p k b t", t=ST)
                chain.link(V.tensor_tensor(by_seq, by_seq, seq_cols(gain), ALU.mult))
                V.tensor_tensor(by_seq, by_seq, seq_cols(modT[:, sh]), ALU.add).then_inc(s_sm, 1)

            def norm_samples_lo(n):
                dve.wait_ge(s_smh, n + 1)
                V.tensor_tensor(samples_of(Xl), samp[:, :, :].rearrange("p k (h c) -> p k h c", h=2),
                                samples_of(Xh).bitcast(F32), ALU.subtract)

            def norm_apply(n, layer, which):
                sh = layer * NMOD + 3 * which
                norm_gain(n, layer, which)
                norm_diag(n)
                packed = samp[:, :, :].rearrange("p k (h c) -> p k h c", h=2)
                by_seq = samp[:, :, :].rearrange("p k (b t) -> p k b t", t=ST)
                chain.link(V.tensor_copy(packed, samples_of(xT)))
                chain.link(V.tensor_tensor(by_seq, by_seq, seq_cols(gain), ALU.mult))
                dve.wait_ge(s_root, n + 1)

                def scaled(k):
                    if k >= 2:
                        dve.wait_ge(s_kx, X_OF[n] + k - 1)
                    V.scalar_tensor_tensor(prompt(hb[k % 2][:, :]), prompt(xT[:, k, :]), gain[:, k, 0:1],
                                           rstd[:, :, 0:PH], ALU.mult, ALU.mult).then_inc(s_hh, 1)

                scaled(0)
                chain.link(V.tensor_tensor(packed, packed, rstd[:, :, PH:HALF].unsqueeze(1).broadcast_to((P, KT, 2, SH)), ALU.mult))
                V.tensor_tensor(by_seq, by_seq, seq_cols(modT[:, sh]), ALU.add).then_inc(s_sm, 1)
                for k in range(KT):
                    if k:
                        if k + 1 < KT:
                            scaled(k + 1)
                    else:
                        norm_samples_lo(n)
                    dve.wait_ge(s_hhi, KT * n + k + 1)
                    V.scalar_tensor_tensor(prompt(Xl[:, k, :]), prompt(hb[k % 2][:, :]), modT[:, sh, k, 0:1],
                                           prompt(Xh[:, k, :].bitcast(F32)), ALU.add, ALU.subtract).then_inc(s_kx, 1)
                    if k == 0:
                        scaled(1)

            dve.wait_ge(s_silu, 1)
            chain.link(V.tensor_scalar(cexp[:, :, :], cexp[:, :, :], 1.0, None, ALU.add))
            chain.link(V.reciprocal(ccol[:, :, :], cexp[:, :, :]))
            chain.link(V.tensor_tensor(ccol[:, :, :], B5[:, 0:KT * NSEQ].rearrange("p (k c) -> p k c", k=KT), ccol[:, :, :], ALU.mult))
            chain.link(V.tensor_copy(c2[:, :, 0:NSEQ], ccol[:, :, :]))
            V.tensor_tensor(c2[:, :, NSEQ:2 * NSEQ], ccol[:, :, :], c2[:, :, 0:NSEQ].bitcast(F32), ALU.subtract)\
                .then_inc(s_cs, 1)
            for n, t0 in enumerate((T_ADA0, T_ADA1)):
                for t in range(t0, t0 + KT, 2):
                    pair = t // 2
                    dve.wait_ge(s_hi, t + 1)
                    V.tensor_tensor(wl[:, t % SLOTS], raw_of(t), wh[:, t % SLOTS].bitcast(F32), ALU.subtract)\
                        .then_inc(s_lo[0], 1)
                    if pair == 2:
                        dve.wait_ge(s_pt, 1)
                        V.tensor_copy(par0[:, :], B7[:, 0:P])
                        V.tensor_copy(par1[:, :], B7[:, P:P + 40]).then_inc(s_ptd, 1)
                        dve.wait_ge(s_ptd, 1)
                    if pair == 1:
                        dve.wait_ge(s_xst, 1)
                        V.tensor_copy(samples_of(xT), B6[:, 0:KT * NS].rearrange("p (k h c) -> p k h c", k=KT, h=2))\
                            .then_inc(s_xse, 1)
                        dve.wait_ge(s_xse, 1)
                    for k in X_AFTER.get(pair - 1, ()):
                        dve.wait_ge(s_xe, k + 1)
                        squares(k, 0)
                    if pair == 5:
                        norm_diag(0)
                    if pair >= 6:
                        dve.wait_ge(s_root, 1)
                        for k in range(4 * (pair - 6), 4 * (pair - 5)):
                            V.tensor_tensor(prompt(xn[:, k, :]), prompt(xT[:, k, :]), rstd[:, :, 0:PH], ALU.mult)
                    if pair == 7:
                        dve.wait_ge(s_gs, 1)
                        V.tensor_tensor(gl[:, :, :], graw[:, :, :], gh[:, :, :].bitcast(F32), ALU.subtract).then_inc(s_gs, 1)
                        chain.link(V.tensor_tensor(samp[:, :, :].rearrange("p k (h c) -> p k h c", h=2), samples_of(xT),
                                                   rstd[:, :, PH:HALF].unsqueeze(1).broadcast_to((P, KT, 2, SH)), ALU.mult))
                combine(n, n, n * KT)
                if n == 1:
                    norm_gain(0, 0, 0)
            norm_samples(0, 0, 0)
            norm_samples_lo(0)
            for k in range(KT):
                if k >= 2:
                    dve.wait_ge(s_kx, X_NORM0 + k - 1)
                chain.link(V.tensor_scalar(prompt(hb[k % 2][:, :]), prompt(xn[:, k, :]), gain[:, k, 0:1],
                                           modT[:, 0, k, 0:1], ALU.mult, ALU.add))
                dve.wait_ge(s_hhi, k + 1)
                V.tensor_tensor(prompt(Xl[:, k, :]), prompt(hb[k % 2][:, :]), prompt(Xh[:, k, :].bitcast(F32)),
                                ALU.subtract).then_inc(s_kx, 1)
            dve.wait_ge(s_gp, 1)
            dve.wait_ge(s_gin, 80)
            R = [r[:, :] for r in rows]
            lf = sqb[0:H, :]
            for hf, bank in enumerate((B5, B7)):
                cols = slice(hf * HALF, (hf + 1) * HALF)
                V.tensor_scalar(R[3][:, cols], bank[0:H, 0:HALF], bgate[0:H, :], None, ALU.add)
                V.tensor_scalar(R[4][:, cols], bank[32:32 + H, 0:HALF], bgate[32:32 + H, :], None, ALU.add)
            chain.link(V.memset(xr[0:H, :], 1.0))
            V.scalar_tensor_tensor(R[0], R[4], -1.0, R[4], ALU.mult, ALU.max).then_inc(s_rv, 1)
            dve.wait_ge(s_ra, 1)
            chain.link(V.scalar_tensor_tensor(lf, R[4], 0.0, R[2], ALU.min, ALU.subtract))
            chain.link(V.tensor_tensor_scan(R[1][:, 0:PH], xr[0:H, 0:PH], lf[:, 0:PH], 0.0, ALU.mult, ALU.add))
            chain.link(V.tensor_tensor_scan(R[1][:, HALF:HALF + PH], xr[0:H, 0:PH], lf[:, HALF:HALF + PH],
                                            R[1][:, PH - 1:PH], ALU.mult, ALU.add))
            S4 = [sample4(r) for r in R]
            chain.link(V.tensor_copy(S4[1][:, :, :, 0], sample4(lf)[:, :, :, 0]))
            for t in range(1, ST):
                chain.link(V.tensor_tensor(S4[1][:, :, :, t], S4[1][:, :, :, t - 1], sample4(lf)[:, :, :, t], ALU.add))
            chain.link(V.tensor_tensor(R[3], R[3], R[1], ALU.subtract))
            chain.link(V.tensor_tensor_scan(R[2][:, 0:PH], xr[0:H, 0:PH], R[3][:, 0:PH], 0.0, ALU.mult, ALU.max))
            chain.link(V.tensor_tensor_scan(R[2][:, HALF:HALF + PH], xr[0:H, 0:PH], R[3][:, HALF:HALF + PH],
                                            R[2][:, PH - 1:PH], ALU.mult, ALU.max))
            m0 = m0row[:, :].rearrange("h (a b) -> h a b", a=2)
            for t in range(ST):
                chain.link(V.tensor_tensor(S4[2][:, :, :, t], S4[2][:, :, :, t - 1] if t else m0, S4[3][:, :, :, t], ALU.max))
            V.tensor_tensor(R[0], R[1], R[2], ALU.add)
            V.tensor_scalar(R[4], R[2], -1.0, None, ALU.mult).then_inc(s_rv, 1)
            dve.wait_ge(s_rv, 2)
            spread = lambda ap: ap.unsqueeze(3).broadcast_to((H, 2, ST, ST))
            dve.wait_ge(s_ra, 2)
            V.tensor_tensor(S4[1], S4[3], spread(S4[4][:, :, :, ST - 1]), ALU.add)
            V.tensor_tensor(S4[2], S4[4], spread(m0), ALU.add)
            dve.wait_ge(s_kx, X_NORM0 + KT)
            V.tensor_copy(negMp[:, :].rearrange("h (a c) -> h a c", a=2), prompt(R[4])).then_inc(s_rv, 1)
            V.memset(vtok[:, :, :, DV:DVA], 1.0)
            nvt = {"n": 0}

            def turned(dst, dst_s):
                nvt["n"] += 1
                dve.wait_ge(s_vt, nvt["n"])
                V.tensor_copy(dst, B7[:, :].rearrange("p (j c) -> p j c", j=NJ))
                V.tensor_copy(dst_s, B5[0:NS, 0:P]).then_inc(s_vtd, 1)

            dve.wait_ge(s_ra, 3)
            dve.wait_ge(s_tt, 1)
            V.tensor_copy(tok[:, :, :, :], B7[:, 0:3 * NJ * H].rearrange("p (a j h) -> p a j h", a=3, j=NJ)).then_inc(s_ttd, 1)
            dve.wait_ge(s_spill, 16)
            for m in range(KT):
                g = G_QK + m
                dve.wait_ge(s_ev, g + 1)
                src, dst = (qT, qs) if m < 4 else (kT, ks)
                V.tensor_copy(dst[:, m % 4, :].rearrange("p (h c) -> p h c", h=2), sample(src[:, m % 4, :])).then_inc(s_dr, 1)
                if m >= 5:
                    n = m - 5
                    turned(ktok[:, :, n * P:(n + 1) * P], ktok_s[:, n * P:(n + 1) * P])
            turned(ktok[:, :, 3 * P:4 * P], ktok_s[:, 3 * P:4 * P])
            combine(2, 2, 2 * KT)
            for m in range(KT):
                nvt["n"] += 1
                dve.wait_ge(s_vt, nvt["n"])
                V.tensor_copy(vtok[:, :, m, 0:DV], B7[:, :].rearrange("p (j c) -> p j c", j=NJ))
                V.tensor_copy(vtok_s[:, m, 0:DV], B5[0:NS, 0:P]).then_inc(s_dr, 1)
            combine(3, 3, 3 * KT)
            dve.wait_ge(s_dr, G_O)
            KS = DK ** -0.5
            chain.link(V.tensor_scalar(tok[:, 1, :, :], tok[:, 1, :, :], KS, None, ALU.mult))
            dve.wait_ge(s_bi, 16 * 7)
            chain.link(V.tensor_scalar(a_s[:, :], a_s[:, :], KS, None, ALU.mult))
            for jt in range(NJ):
                kv = ktok[:, jt, :].rearrange("p (h d) -> p h d", h=H)
                V.tensor_tensor(kv, kv, tok[:, 1, jt, :].unsqueeze(2).broadcast_to((P, H, DK)), ALU.mult)
            kv = ktok_s[:, :].rearrange("p (h d) -> p h d", h=H)
            chain.link(V.tensor_tensor(kv, kv, a_s[:, :].unsqueeze(2).broadcast_to((NS, H, DK)), ALU.mult))
            chain.link(V.tensor_tensor(dec_s[:, :, :], negM_s[:, :, :], g_s[:, :].unsqueeze(2).broadcast_to((NS, H, NS)), ALU.add))
            V.tensor_scalar(dec_s[:, :, :], dec_s[:, :, :], 0.0, None, ALU.min).then_inc(s_sp, 1)
            dve.wait_ge(s_srs, 1)
            chain.link(V.tensor_tensor(sqb[:, 0:H // 2 * NS].rearrange("p (a t) -> p a t", a=H // 2), qs[:, :, :], einter_s[:, :, :], ALU.mult))
            qe = sqb[:, 0:H // 2 * NS].rearrange("p (a t) -> p a t", a=H // 2)
            for h2 in range(2):
                pr = slice(DK * h2, DK * (h2 + 1))
                for b in range(SB):
                    last = V.tensor_copy(qbd[pr, :, b, NS * h2 + ST * b:NS * h2 + ST * (b + 1)], qe[pr, :, ST * b:ST * (b + 1)])
            last.then_inc(s_sp, 1)
            def update_state(a):
                for b in range(SB):
                    n = SB * a + b
                    dve.wait_ge(s_cu, n + 1)
                    bank = (B5, B7)[n % 2]
                    for h2 in range(2):
                        pr = slice(DK * h2, DK * (h2 + 1))
                        last = V.scalar_tensor_tensor(C0[pr, b, a, :], C0[pr, b, a, :],
                                                      einter_s[pr, a, ST * b + ST - 1:ST * b + ST],
                                                      bank[pr, h2 * DVA:(h2 + 1) * DVA], ALU.mult, ALU.add)
                    last.then_inc(s_cud if n == SB * H // 2 - 1 else s_upd, 1)

            def drain_gate(m, g, j, per):
                dve.wait_ge(s_ev, g + 1)
                s = stage[g % 2][:, :]
                chain.link(V.tensor_scalar(s, s, 1.0, None, ALU.add))
                chain.link(V.reciprocal(sqb[:, :], s))
                V.tensor_scalar(og[:, m, :], sqb[:, :], par1[:, 8 + m:9 + m], None, ALU.mult).then_inc(s_dr, 1)
                if STATE_TILE - 1 <= m < STATE_TILE - 1 + H // 2:
                    update_state(m - STATE_TILE + 1)

            unit(G_O, drain_gate, low=T_O + 15)
            combine(4, 4, 4 * KT)
            dve.wait_ge(s_ssc, 1)
            dve.wait_ge(s_srs, 4)
            for h2 in range(2):
                pick = lambda ap: ap.rearrange("p (a h) t -> p a h t", h=2)[:, :, h2, :]
                last = V.scalar_tensor_tensor(
                    pick(probs_s[:, :, :])[:, :, NS * h2:NS * (h2 + 1)],
                    (B7, B6)[h2][0:NS, 0:H // 2 * NS].rearrange("p (a t) -> p a t", t=NS), KS,
                    pick(dec_s[:, :, :]), ALU.mult, ALU.mult)
            last.then_inc(s_sp, 1)

            def head_norm(nm, npart, enm, w, ssq, sq_sem, rs_n, hs_out, out_sem, meanwhile=None):
                st = [stat[0:npart, i, 0:w] for i in range(5)]
                den = nm[:, :, DV]
                chain.link(V.scalar_tensor_tensor(st[0], den, -1.0, den, ALU.mult, ALU.max))
                chain.link(V.tensor_tensor(st[0], st[0], enm, ALU.max))
                chain.link(V.reciprocal(st[1], st[0]))
                ssq()
                chain.link(V.tensor_tensor(st[4], st[4], st[1], ALU.mult))
                V.tensor_scalar(st[2], st[4], 1.0 / DV, EPS, ALU.mult, ALU.add).then_inc(sq_sem, 1)
                if meanwhile is not None:
                    meanwhile()
                dve.wait_ge(s_rs, rs_n)
                chain.link(V.tensor_tensor(st[0], st[1], st[3], ALU.mult))
                V.tensor_tensor(hs_out, nm[:, :, 0:DV], st[0].unsqueeze(2).broadcast_to((npart, w, DV)), ALU.mult).then_inc(out_sem, 1)

            dve.wait_ge(s_spv, 1)
            dve.wait_ge(s_oldout, 1)
            V.tensor_tensor(num_s[:, :, :], num_s[:, :, :], G[0:2 * NS, :, 0:DVA], ALU.add).then_inc(s_snum, 1)
            dve.wait_ge(s_snum, 1)

            def sample_ssq():
                sq = stage[0][0:2 * NS, :][:, 0:H // 2 * DV].rearrange("p (j e) -> p j e", e=DV)
                chain.link(V.tensor_tensor(sq, num_s[:, :, 0:DV], num_s[:, :, 0:DV], ALU.mult))
                chain.link(V.tensor_reduce(stat[0:2 * NS, 4, :], sq, AX.X, ALU.add))
                chain.link(V.tensor_tensor(stat[0:2 * NS, 4, :], stat[0:2 * NS, 4, :], stat[0:2 * NS, 1, :], ALU.mult))

            head_norm(num_s[:, :, :], 2 * NS, enm_s[:, :], H // 2, sample_ssq, s_sp, 1, hs[0:2 * NS, :, :], s_sp)
            dve.wait_ge(s_sht, 1)
            V.tensor_tensor(og[:, :, :].rearrange("p k (h c) -> p k h c", h=2)[:, :, :, PH:HALF],
                            og[:, :, :].rearrange("p k (h c) -> p k h c", h=2)[:, :, :, PH:HALF],
                            B6[:, 0:H * NS].rearrange("p (k h c) -> p k h c", k=H, h=2), ALU.mult).then_inc(s_sp, 1)
            def gated(g):
                dve.wait_ge(s_ht, g + 1)
                V.tensor_tensor(prompt(og[:, g, :]), prompt(og[:, g, :]), B5[:, :].rearrange("p (h c) -> p h c", h=2),
                                ALU.mult).then_inc(s_y, 1)
                dve.wait_ge(s_y, g + 1)
                V.tensor_copy(Xh[:, g, :], og[:, g, :]).then_inc(s_yh, 1)

            for h in range(H + 1):
                if h < H:
                    o = 0
                    for i in range(NJ):
                        w = SEQ - P * i
                        dve.wait_ge(s_s, NJ * h + i + 1)
                        dve.wait_ge(s_sel, NJ * h + i + 1)
                        pr = probs[h % 2][:, o:o + w]
                        V.scalar_tensor_tensor(pr, G[:, i, 0:w], KS, pr, ALU.mult, ALU.mult).then_inc(s_pr, 1)
                        o += w
                if 1 <= h <= H:
                    g = h - 1
                    dve.wait_ge(s_num, g + 1)
                    if g:
                        dve.wait_ge(s_ht, g)
                    else:
                        dve.wait_ge(s_sht, 1)

                    def prompt_ssq():
                        dve.wait_ge(s_ssq, g + 1)
                        chain.link(V.tensor_tensor(stat[:, 4, :], stat[:, SSQ + g % 2, :], stat[:, 1, :], ALU.mult))

                    head_norm(num[g % 2][:, :, :], P, tok[:, 2, :, g], NJ, prompt_ssq, s_sq, g + 2, hs[:, :, :], s_hs,
                              (lambda: gated(g - 1)) if g else None)
            gated(H - 1)
            dve.wait_ge(s_back, 16 * KT)
            dve.wait_ge(s_out, 16 * STORES_STATE)
            dve.wait_ge(s_mod, 3)
            unit(G_WOUT, residual(2, 1), low=T_WOUT + 15)
            combine(5, 5, 5 * KT)
            norm_apply(1, 0, 1)
            dve.wait_ge(s_mod, 6)
            start = mids["n"]
            with dve.Fori(0, QUARTERS - 1) as j:
                unit(G_MLP0, drain_square(Hh, Hl, None), j, 16, T_MLP0 + 15, 32)
                combine(6, j + NMOD, j * KT + 6 * KT, j, 2)
                unit(G_MLP0 + 8, residual(5), j, 16, T_MLP0 + 31, 32)
                combine(7, j + (NMOD + 3), j * KT + 9 * KT, j, 2)
            assert mids["n"] - start == 16
            mids["n"] = start + 16 * (QUARTERS - 1)
            unit(G_MLP0_LAST, drain_square(Hh, Hl, None))
            unit(G_MLP0_LAST + 8, residual(5, 2))
            norm_apply(2, 1, 0)
            for m in range(KT):
                dve.wait_ge(s_ev, G_CG + m + 1)
                dve.wait_ge(s_dr, G_CG + m)
                V.memset(small_s[:, 0:1], 0.0).then_inc(s_dr, 1)
            dve.wait_ge(s_cre, 2)
            cw = lambda w, m: par1[:, 16 + w * KT + m:17 + w * KT + m]
            for m in range(KT):
                g = G_XT + m
                dve.wait_ge(s_ev, g + 1)
                dve.wait_ge(s_dr, g)
                s = stage[g % 2][:, :]
                up = u[:, m, 0:2 + SEQ]
                us = u[:, m, 2 + SEQ:UROW].rearrange("p (b t) -> p b t", t=2 + ST)
                V.tensor_tensor(up[:, 2:2 + SEQ].rearrange("p (h c) -> p h c", h=2),
                                up[:, 2:2 + SEQ].rearrange("p (h c) -> p h c", h=2), prompt(s), ALU.mult)
                us4 = us.rearrange("p (h b) t -> p h b t", h=2)
                chain.link(V.tensor_tensor(us4[:, :, :, 2:2 + ST], us4[:, :, :, 2:2 + ST], sample4(s), ALU.mult))
                yp = prompt(yc[:, m, :])
                ys = sample4(yc[:, m, :])
                ph = lambda w: up[:, w:w + SEQ].rearrange("p (h c) -> p h c", h=2)
                V.tensor_scalar(yp, ph(0), cw(0, m), None, ALU.mult)
                tmp = small_s[:, :].rearrange("p (b t) -> p b t", t=ST)
                chain.link(V.tensor_scalar(tmp, us[:, :, 0:ST], cw(0, m), None, ALU.mult))
                for w in (1, 2):
                    V.scalar_tensor_tensor(yp, ph(w), cw(w, m), yp, ALU.mult, ALU.add)
                    chain.link(V.scalar_tensor_tensor(tmp, us[:, :, w:w + ST], cw(w, m), tmp, ALU.mult, ALU.add))
                V.tensor_copy(sample(yc[:, m, :]), small_s[:, :].rearrange("p (h c) -> p h c", h=2))
                V.tensor_copy(ulast[:, m, 0:2], up[:, SEQ:SEQ + 2])
                V.tensor_copy(ulast[:, m, 2:2 * NSEQ].rearrange("p (b r) -> p b r", r=2), us[:, :, ST:ST + 2])\
                    .then_inc(s_dr, 1)
            dve.wait_ge(s_dr, G_BG)
            unit(G_BG, drain_square(Hh, Hl, yc))
            unit(G_COUT, residual(NMOD + 2, 3))
            norm_apply(3, 1, 1)
            start = mids["n"]
            with dve.Fori(0, QUARTERS - 1) as j:
                unit(G_MLP1, drain_square(Hh, Hl, None), j, 16)
                unit(G_MLP1 + 8, residual(NMOD + 5), j, 16)
            assert mids["n"] - start == 16
            mids["n"] = start + 16 * (QUARTERS - 1)
            unit(G_MLP1_LAST, drain_square(Hh, Hl, None))
            unit(G_MLP1_LAST + 8, residual(NMOD + 5, 4))
            norm_diag(4)
            dve.wait_ge(s_root, 5)
            for m in range(KT):
                if m >= 2:
                    dve.wait_ge(s_ft, m - 1)
                V.scalar_tensor_tensor(halves(hb[m % 2][:, :]), halves(xT[:, m, :]), par1[:, m:m + 1], rstd, ALU.mult, ALU.mult)\
                    .then_inc(s_fy, 1)

        @block.tensor
        def _(pe):
            mm = nc.tensor.matmul

            def turn(out, in_, n):
                return nc.tensor.transpose(out, in_, ident[0:n, 0:n])

            def tile(t, g, xh, xl, j, per_t, per_g, between=None, before_last=None):
                s = t % SLOTS
                split_wait(pe, t, j, per_t)
                if g >= 2:
                    pe.wait_ge(s_ev, at(g - 1, j, per_g))
                for k in range(KT):
                    first, final = k == 0, k == KT - 1
                    if final and before_last is not None:
                        before_last()
                    for w, x, st, en in ((wh, xh, first, False), (wh, xl, False, False), (wl, xh, False, final)):
                        for hf in range(2):
                            last = mm(G[:, 2 * (g % 2) + hf, 0:HALF], w[:, s, k, :], x[:, k, hf * HALF:(hf + 1) * HALF],
                                      start=st, stop=en)
                    if final:
                        last.then_inc(s_used, 1)
                    if between is not None:
                        between(k)

            def tile_pair(t, g, xh, xl, j, per_t, per_g, ready):
                ahead = 5
                for k, o in (*((k, o) for k in range(ahead) for o in range(2)),
                             *((k, o) for o in range(2) for k in range(ahead, KT))):
                    if k == 0:
                        split_wait(pe, t + o, j, per_t)
                        if g + o >= 2:
                            pe.wait_ge(s_ev, at(g + o - 1, j, per_g))
                    if o == 0:
                        ready(k)
                    s, q = (t + o) % SLOTS, 2 * ((g + o) % 2)
                    first, final = k == 0, k == KT - 1
                    for w, x, st, en in ((wh, xh, first, False), (wh, xl, False, False), (wl, xh, False, final)):
                        for hf in range(2):
                            last = mm(G[:, q + hf, 0:HALF], w[:, s, k, :], x[:, k, hf * HALF:(hf + 1) * HALF],
                                      start=st, stop=en)
                    if final:
                        last.then_inc(s_used, 1)

            def ada_pair(t, k, j=None, per_t=0, per_k=0):
                split_wait(pe, t, j, per_t)
                split_wait(pe, t + 1, j, per_t)
                if k >= 1:
                    pe.wait_ge(s_ae, at(k, j, per_k))
                s = t % SLOTS
                for kk in range(KT):
                    for w in (wh, wl):
                        last = mm(B4[0:2 * NSEQ, 0:2 * P], c2[:, kk, :], w[:, s:s + 2, kk, :],
                                  start=(kk == 0 and w is wh), stop=(kk == KT - 1 and w is wl))
                last.then_inc(s_used, 2)

            def ada_turn(n, j=None, per=0):
                if j is None:
                    pe.wait_ge(s_ae, 4 * (n + 1))
                for m in range(KT):
                    last = turn(B6[:, m * 2 * NSEQ:(m + 1) * 2 * NSEQ], modrow[:, m * P:(m + 1) * P], 2 * NSEQ)
                last.then_inc(s_tr, 1)

            def unit(t0, g0, xh, xl, j=None, per_t=0, per_g=0, ready=None):
                tile_pair(t0, g0, xh, xl, j, per_t, per_g, ready)
                for m in range(2, KT):
                    tile(t0 + m, g0 + m, xh, xl, j, per_t, per_g)

            def mixed(t0, g0, n, xh, xl, ready, j=None, per_t=0, per_g=0, per_n=0, post=None, between=None):
                for o, m, *pair in MIXED:
                    t = t0 + o
                    if m is None:
                        ada_pair(t, 4 * n + pair[0], j, per_t, 4 * per_n)
                        continue
                    if m == 0 and ready is not None:
                        tile_pair(t, g0, xh, xl, j, per_t, per_g, ready)
                    if m <= 1 and ready is not None:
                        continue
                    row_out = None
                    if j is not None and m == KT - 1:
                        row_out = lambda: pe.wait_ge(s_ae, at(4 * (n + 1), j, 4 * per_n))
                    tile(t, g0 + m, xh, xl, j, per_t, per_g, None if between is None else between(m), row_out)
                    if post is not None:
                        post(m)
                ada_turn(n, j, per_n)

            def stats(n):
                pe.wait_ge(s_acc, n + 1)
                pe.wait_ge(s_at, (1, 6, 12, 12, 12)[n])
                for jt, c in enumerate((*range(0, NJ * P, P), TOK - P)):
                    last = mm(B6[:, SUMS + jt:SUMS + jt + 1], acc[:, c:c + P], ones[:, 0:1], start=True, stop=True)
                last.then_inc(s_sum, 1)

            def spread(n):
                pe.wait_ge(s_diag, n + 1)
                for bank, c, jt, o, w in ((B5, 0, 0, 0, P), (B5, P, 1, 0, P), (B5, 2 * P, 2, 0, SH),
                                          (B7, 0, 2, SH, P - SH), (B7, P - SH, 3, 0, P),
                                          (B7, 2 * P - SH, 4, P - 2 * SH, 2 * SH)):
                    last = mm(bank[:, c:c + w], ones[:, :], diag[:, jt, o:o + w], start=True, stop=True)
                last.then_inc(s_root, 1)

            def x_ready(x0):
                return lambda k: pe.wait_ge(s_kx, x0 + k + 1)

            def drained(g0, j=None, per=0):
                return lambda k: pe.wait_ge(s_dr, at(g0 + k + 1, j, per))

            pe.wait_ge(s_const, 1)
            pe.wait_ge(s_cin, 32)
            for k in range(KT):
                last = turn(B5[:, k * NSEQ:(k + 1) * NSEQ], crow[:, k * P:(k + 1) * P], NSEQ)
            last.then_inc(s_ct, 1)
            pe.wait_ge(s_cs, 1)
            for n, t0 in enumerate((T_ADA0, T_ADA1)):
                for m in range(0, KT, 2):
                    pair = (t0 + m) // 2
                    ada_pair(t0 + m, pair)
                    if pair == 1:
                        pe.wait_ge(s_pin, 80)
                        turn(B7[:, 0:P], parrow0[:, :], P)
                        turn(B7[:, P:P + 40], parrow1[:, :], 40).then_inc(s_pt, 1)
                    if pair == 0:
                        pe.wait_ge(s_xin, 80)
                        for k in range(KT):
                            last = turn(B6[:, k * NS:(k + 1) * NS], xin[0:NS, NJ, k * P:(k + 1) * P], NS)
                        last.then_inc(s_xst, 1)
                    for k in X_AFTER.get(pair, ()):
                        if k >= 4:
                            pe.wait_ge(s_xe, k - 3)
                        for jt in range(NJ):
                            last = turn(G[:, k % 4, jt * P:(jt + 1) * P], xin[:, jt, k * P:(k + 1) * P], P)
                        last.then_inc(s_xt, 1)
                    if pair == 4:
                        pe.wait_ge(s_ptd, 1)
                        stats(0)
                    if pair == 5:
                        spread(0)
                if n == 0:
                    pe.wait_ge(s_xse, 1)
                ada_turn(n)
            pe.wait_ge(s_gs, 2)
            pe.wait_ge(s_xe, KT)
            for k in range(KT):
                pe.wait_ge(s_kx, X_NORM0 + k + 1)
                for w, x, st, en in ((gh, Xh, k == 0, False), (gh, Xl, False, False), (gl, Xh, False, k == KT - 1)):
                    for hf, bank in enumerate((B5, B7)):
                        last = mm(bank[0:40, 0:HALF], w[:, k, :], x[:, k, hf * HALF:(hf + 1) * HALF], start=st, stop=en)
            last.then_inc(s_gp, 1)

            def post_k(m):
                if m == 3:
                    pe.wait_ge(s_ra, 3)
                    pe.wait_ge(s_rv, 3)
                    for i, r in enumerate((3, 1, 5)):
                        for jt in range(NJ):
                            c = (i * NJ + jt) * H
                            last = turn(B7[:, c:c + H], rows[r][:, col(jt * P):col(jt * P) + P], H)
                    last.then_inc(s_tt, 1)
                if m >= 5:
                    turn_k(m - 5)
                if m == 7:
                    turn_k(3)

            nt = {"n": 0}

            def turned_free():
                n = nt["n"]
                if n == 0:
                    pe.wait_ge(s_ttd, 1)
                elif n <= 4:
                    pe.wait_ge(s_vtd, n)
                else:
                    pe.wait_ge(s_dr, G_V + n - 4)
                nt["n"] += 1

            def turn_k(n):
                pe.wait_ge(s_dr, G_QK + 4 + n + 1)
                turned_free()
                for jt in range(NJ):
                    turn(B7[:, jt * P:(jt + 1) * P], kT[:, n, col(jt * P):col(jt * P) + P], P)
                turn(B5[0:NS, 0:P], ks[:, n, :], P).then_inc(s_vt, 1)

            def turn_v(m):
                pe.wait_ge(s_ev, G_V + m + 1)
                turned_free()
                st_ = stage[(G_V + m) % 2]
                for jt in range(NJ):
                    turn(B7[:, jt * P:(jt + 1) * P], st_[:, col(jt * P):col(jt * P) + P], P)
                turn(B5[0:NS, 0:P], vs[(G_V + m) % 2][:, :], P).then_inc(s_vt, 1)

            def post_v(m):
                if m >= 1:
                    turn_v(m - 1)
                if m == KT - 1:
                    turn_v(m)

            mixed(T_QK, G_QK, 2, Xh, Xl, None, post=post_k)
            mixed(T_V, G_V, 3, Xh, Xl, None, post=post_v)
            def post_o(m):
                if m != 2:
                    return
                pe.wait_ge(s_sin, 16 * 2 * (SB + 1))
                pe.wait_ge(s_sp, 2)
                pe.wait_ge(s_dr, G_O)
                for a in range(H // 2):
                    out = B5[0:2 * NS, a * DVA:(a + 1) * DVA] if a < 3 else B7[0:2 * NS, 0:DVA]
                    for b in range(SB):
                        last = mm(out, qbd[:, a, b, :], C0[:, b, a, :], start=(b == 0), stop=(b == SB - 1))
                last.then_inc(s_old, 1)

            def state_products(m):
                a = m - STATE_TILE
                if not 0 <= a < H // 2:
                    return None

                def between(k):
                    for b in {2: (0,), 3: (1,), 4: (2,), 5: (3, 4), 6: (5, 6), 7: (7,)}.get(k, ()):
                        n = SB * a + b
                        if b == 0:
                            pe.wait_ge(s_kam, a + 1)
                        if n < 2:
                            pe.wait_ge(s_oldout, 1)
                        else:
                            pe.wait_ge(s_upd, n - 1)
                        mm((B5, B7)[n % 2][:, 0:2 * DVA], kam[a % 2][:, b, :],
                           vtok_s[:, 2 * a:2 * a + 2, :].rearrange("p h e -> p (h e)"), start=True, stop=True).then_inc(s_cu, 1)
                return between

            mixed(T_O, G_O, 4, Xh, Xl, None, post=post_o, between=state_products)
            pe.wait_ge(s_cud, 1)
            pe.wait_ge(s_at, 5)
            for h in (*range(0, H, 2), *range(1, H, 2)):
                pr = slice(DK * (h % 2), DK * (h % 2) + DK)
                last = mm((B7, B6)[h % 2][0:NS, h // 2 * NS:(h // 2 + 1) * NS], ks[pr, h // 2, :], qs[pr, h // 2, :], start=True, stop=True)
            last.then_inc(s_ssc, 1)
            pe.wait_ge(s_ev, G_WOUT)
            pe.wait_ge(s_sp, 3)
            for a in range(H // 2):
                for h2 in range(2):
                    last = mm(G[0:2 * NS, a, 0:DVA], probs_s[:, 2 * a + h2, :], vtok_s[:, 2 * a + h2, :],
                              start=(h2 == 0), stop=(h2 == 1))
            last.then_inc(s_spv, 1)
            pe.wait_ge(s_selr, 1)
            pe.wait_ge(s_snum, 1)
            for h in range(H + 2):
                if h < H:
                    hm, pr = h // 2, slice(DK * (h % 2), DK * (h % 2) + DK)
                    if h:
                        pe.wait_ge(s_d, NJ * h)
                    mm(B4[:, :], sel[:, h, :], negMp[:, :], start=True, stop=True).then_inc(s_bc, 1)
                    for i in range(NJ):
                        if h:
                            pe.wait_ge(s_pr, NJ * (h - 1) + i + 1)
                        t0 = P * i
                        for hf in range(2):
                            lo_, hi_ = max(t0, PH * hf), PH * (hf + 1)
                            if lo_ < hi_:
                                last = mm(G[:, i, lo_ - t0:hi_ - t0], kT[pr, hm, col(t0):col(t0) + P],
                                          qT[pr, hm, col(lo_):col(lo_) + hi_ - lo_], start=True, stop=True)
                        last.then_inc(s_s, 1)
                if h == 0:
                    pe.wait_ge(s_sp, 5)
                    pe.wait_ge(s_at, 5)
                    for a in range(H // 2):
                        last = turn(B6[:, a * 2 * NS:(a + 1) * 2 * NS], hs[0:2 * NS, a, :], 2 * NS)
                    last.then_inc(s_sht, 1)
                if 1 <= h <= H:
                    g = h - 1
                    pe.wait_ge(s_pr, NJ * (g + 1))
                    if g:
                        pe.wait_ge(s_num, g)
                    else:
                        pe.wait_ge(s_sp, 6)
                    for jt in range(NJ):
                        out = (B6, B7)[jt // 2][:, (jt % 2) * DVA:(jt % 2 + 1) * DVA]
                        o = 0
                        for i in range(jt + 1):
                            c = o + P * (jt - i)
                            last = mm(out, probs[g % 2][:, c:c + P], vtok[:, i, g, :], start=(i == 0), stop=(i == jt))
                            o += SEQ - P * i
                    last.then_inc(s_pv, 1)
                if h >= 2:
                    g = h - 2
                    pe.wait_ge(s_hs, g + 1)
                    if g:
                        pe.wait_ge(s_y, g)
                    for jt in range(NJ):
                        last = turn(B5[:, jt * P:(jt + 1) * P], hs[:, jt, :], P)
                    last.then_inc(s_ht, 1)
            for h in range(H):
                for i in range(NJ):
                    last = mm(G[0:DK, h // 3, (h % 3) * DVA:(h % 3 + 1) * DVA], ktok[:, i, h * DK:(h + 1) * DK],
                              vtok[:, i, h, :], start=(i == 0), stop=(i == NJ - 1))
            last.then_inc(s_cp, 1)
            pe.wait_ge(s_cpo, 1)
            mixed(T_WOUT, G_WOUT, 5, Xh, Xl, x_ready(X_Y))
            stats(1)
            spread(1)
            MLP0_X = x_ready(X_NORM1)
            with pe.Fori(0, QUARTERS - 1) as j:
                mixed(T_MLP0, G_MLP0, 6, Xh, Xl, MLP0_X, j, 32, 16, 2)
                mixed(T_MLP0 + 16, G_MLP0 + 8, 7, Hh, Hl, drained(G_MLP0, j, 16), j, 32, 16, 2)
            unit(T_MLP0_LAST, G_MLP0_LAST, Xh, Xl, ready=MLP0_X)
            unit(T_MLP0_LAST + 8, G_MLP0_LAST + 8, Hh, Hl, ready=drained(G_MLP0_LAST))
            pe.wait_ge(s_crin, 16)
            pe.wait_ge(s_at, 12)
            for k in range(KT):
                last = turn(B6[:, k * 2 * SB:(k + 1) * 2 * SB], crows[:, k * P:(k + 1) * P], 2 * SB)
            last.then_inc(s_crt, 1)
            stats(2)
            spread(2)
            unit(T_CG, G_CG, Xh, Xl, ready=x_ready(X_NORM2))
            unit(T_XT, G_XT, Xh, Xl, ready=x_ready(X_NORM2))
            unit(T_BG, G_BG, Xh, Xl, ready=x_ready(X_NORM2))
            pe.wait_ge(s_dr, G_BG)
            pe.wait_ge(s_cre, 2)
            for k in range(KT):
                last = mm((B4, B6)[k // 4][0:2 * NSEQ, (k % 4) * P:(k % 4 + 1) * P], ulast[:, k, :], ident[:, :],
                          start=True, stop=True, is_transpose=True)
            last.then_inc(s_ult, 1)
            unit(T_COUT, G_COUT, Hh, Hl, ready=drained(G_BG))
            stats(3)
            spread(3)
            MLP1_X = x_ready(X_NORM3)
            with pe.Fori(0, QUARTERS - 1) as j:
                unit(T_MLP1, G_MLP1, Xh, Xl, j, 16, 16, ready=MLP1_X)
                unit(T_MLP1 + 8, G_MLP1 + 8, Hh, Hl, j, 16, 16, ready=drained(G_MLP1, j, 16))
            unit(T_MLP1_LAST, G_MLP1_LAST, Xh, Xl, ready=MLP1_X)
            unit(T_MLP1_LAST + 8, G_MLP1_LAST + 8, Hh, Hl, ready=drained(G_MLP1_LAST))
            stats(4)
            spread(4)
            pe.wait_ge(s_ulo, 1)
            for m in range(KT):
                pe.wait_ge(s_fy, m + 1)
                if m >= 2:
                    pe.wait_ge(s_fo, m - 1)
                hm = hb[m % 2]
                for jt in range(NJ):
                    turn(G[:, m % 4, jt * P:(jt + 1) * P], hm[:, col(jt * P):col(jt * P) + P], P)
                for hf in range(2):
                    c = hf * HALF + PH
                    last = mm((B4, B6)[m % 2][0:SH, hf * P:(hf + 1) * P], hm[:, c:c + SH], ident[:, :],
                              start=True, stop=True, is_transpose=True)
                last.then_inc(s_ft, 1)


STORES_STATE = 2 * (SB + 1) + 2
N_STORES = STORES_STATE + 2 + KT + 1

_INS = ["x_prompt", "x_sample", "c_prompt", "c_sample", "state_mlstm_C", "state_mlstm_n", "state_mlstm_m", "state_conv",
        "ada_w", "ada_b", "norm_g", "final_norm_g", "mlstm_w_in", "mlstm_b_gates", "mlstm_head_g", "mlstm_w_out",
        "conv_w_in", "conv_w", "conv_w_out", "mlp_w_up", "mlp_w_down"]
_OUTS = [(1, SEQ, D), (SB, ST, D), (1, 1, H, DK, DV), (1, 1, H, DK), (1, 1, H), (1, 1, 2, D),
         (1, SB, H, DK, DV), (1, SB, H, DK), (1, SB, H), (1, SB, 2, D)]


def kernel(**inputs):
    import numpy as np
    import concourse.bacc as bacc
    from concourse.bass_utils import run_bass_kernel_spmd

    nc = bacc.Bacc("TRN2", target_bir_lowering=False, num_devices=1)
    arrays, args = {}, {}
    for name in _INS:
        a = np.ascontiguousarray(inputs[name])
        arrays[f"in_{name}"] = a
        args[name] = nc.dram_tensor(f"in_{name}", a.shape, mybir.dt.from_np(a.dtype), kind="ExternalInput").ap()
    outs = [nc.dram_tensor(f"out_{i}", s, F32, kind="ExternalOutput").ap() for i, s in enumerate(_OUTS)]
    build_program(nc, args, outs)
    r = run_bass_kernel_spmd(nc, [arrays], core_ids=[0])
    return tuple(r.results[0][f"out_{i}"] for i in range(len(_OUTS)))
```
